# Optimizing a Trainium2 kernel written in Bass

```python
import math
import jax, jax.numpy as jnp
from jax import lax
import numpy as np

D_MODEL = 1024
BATCH = 1
SEQ = 256
DEPTH = 2
DEC_BATCH = 1
DEC_SEQ = 256
PAST_LEN = 128

HEAD_DIM = 64
N_HEADS_A = 8
N_KV_A = 2
N_HEADS_B = 8
N_KV_B = 2
WIDTH_A = N_HEADS_A * HEAD_DIM
WIDTH_B = N_HEADS_B * HEAD_DIM
KVW_A = N_KV_A * HEAD_DIM
KVW_B = N_KV_B * HEAD_DIM
MIX_WIDTH = WIDTH_A + WIDTH_B
IN_WIDTH = WIDTH_A + 2 * KVW_A + WIDTH_B + 2 * KVW_B
Q_BLOCK = 128
BAND_BLOCK = 128
WINDOW = 128
ROPE_THETA = 10000.0
GRID_W = 64
D_FF = 2816
CONV_W = 3
D_PLE = 256
NORM_EPS = 1e-5
QK_EPS = 1e-6
ALPHA = (2 * DEPTH) ** 0.25
BETA = (8 * DEPTH) ** -0.25

kernel_name = 'hymba_axial_window_sink_encoder'

F32 = jnp.float32

def layer_norm(x, g, b):
    xf = x.astype(F32)
    mu = jnp.mean(xf, -1, keepdims=True)
    var = jnp.mean(jnp.square(xf - mu), -1, keepdims=True)
    return ((xf - mu) * lax.rsqrt(var + NORM_EPS) * g.astype(F32) + b.astype(F32)).astype(x.dtype)

def rms_norm(x, g, eps):
    xf = x.astype(F32)
    return xf * lax.rsqrt(jnp.mean(xf * xf, -1, keepdims=True) + eps) * g.astype(F32)

def rope_angles_1d(n):
    pos = jnp.arange(n, dtype=F32)
    inv = ROPE_THETA ** (-jnp.arange(0, HEAD_DIM, 2, dtype=F32) / HEAD_DIM)
    return pos[:, None] * inv[None, :]

def rope_angles_2d(n):
    rows = n // GRID_W
    row = jnp.repeat(jnp.arange(rows, dtype=F32), GRID_W)
    col = jnp.tile(jnp.arange(GRID_W, dtype=F32), rows)
    axis_dim = HEAD_DIM // 2
    inv = ROPE_THETA ** (-jnp.arange(0, axis_dim, 2, dtype=F32) / axis_dim)
    return jnp.concatenate([row[:, None] * inv[None, :], col[:, None] * inv[None, :]], -1)

def apply_rope(x, ang):
    xf = x.astype(F32).reshape(x.shape[:-1] + (HEAD_DIM // 2, 2))
    c = jnp.cos(ang)[None, :, None, :]
    s = jnp.sin(ang)[None, :, None, :]
    x0, x1 = xf[..., 0], xf[..., 1]
    return jnp.stack([x0 * c - x1 * s, x0 * s + x1 * c], -1).reshape(x.shape)

def global_axial_attention(q, k, v, q_gain, k_gain, ang2d):
    B, S = q.shape[0], q.shape[1]
    G = N_HEADS_A // N_KV_A
    q = apply_rope(rms_norm(q, q_gain, QK_EPS), ang2d) * (HEAD_DIM ** -0.5)
    k = apply_rope(rms_norm(k, k_gain, QK_EPS), ang2d)
    v = v.astype(F32)
    nq = S // Q_BLOCK
    qb = q.reshape(B, nq, Q_BLOCK, N_KV_A, G, HEAD_DIM).transpose(1, 0, 2, 3, 4, 5)

    def attend(qblk):
        s = jnp.einsum('bqkgd,bskd->bkgqs', qblk, k)
        p = jax.nn.softmax(s, axis=-1)
        return jnp.einsum('bkgqs,bskd->bqkgd', p, v)

    o = lax.map(attend, qb)
    return o.transpose(1, 0, 2, 3, 4, 5).reshape(B, S, WIDTH_A)

def window_sink_attention(q, k, v, sink, ang1d):
    B, S = q.shape[0], q.shape[1]
    G = N_HEADS_B // N_KV_B
    BB = BAND_BLOCK
    nb = S // BB
    q = apply_rope(q, ang1d) * (HEAD_DIM ** -0.5)
    k = apply_rope(k, ang1d)
    v = v.astype(F32)
    pad = ((0, 0), (BB, BB), (0, 0), (0, 0))
    kp = jnp.pad(k, pad).reshape(B, nb + 2, BB, N_KV_B, HEAD_DIM)
    vp = jnp.pad(v, pad).reshape(B, nb + 2, BB, N_KV_B, HEAD_DIM)
    kband = jnp.concatenate([kp[:, :-2], kp[:, 1:-1], kp[:, 2:]], axis=2)
    vband = jnp.concatenate([vp[:, :-2], vp[:, 1:-1], vp[:, 2:]], axis=2)
    qb = q.reshape(B, nb, BB, N_KV_B, G, HEAD_DIM)
    a = jnp.arange(BB)[:, None]
    j = jnp.arange(3 * BB)[None, :]
    band = jnp.abs(j - BB - a) <= WINDOW
    sink_l = sink.astype(F32).reshape(1, N_KV_B, G, 1, 1)

    def attend(args):
        blk, qblk, kblk, vblk = args
        kpos = blk * BB - BB + jnp.arange(3 * BB)
        mask = band & ((kpos >= 0) & (kpos < S))[None, :]
        s = jnp.einsum('bqkgd,bskd->bkgqs', qblk, kblk)
        s = jnp.where(mask, s, -jnp.inf)
        m = jnp.maximum(jnp.max(s, -1, keepdims=True), sink_l)
        e = jnp.exp(s - m)
        denom = jnp.sum(e, -1, keepdims=True) + jnp.exp(sink_l - m)
        return jnp.einsum('bkgqs,bskd->bqkgd', e / denom, vblk)

    o = lax.map(attend, (jnp.arange(nb), qb.transpose(1, 0, 2, 3, 4, 5),
                         kband.transpose(1, 0, 2, 3, 4), vband.transpose(1, 0, 2, 3, 4)))
    return o.transpose(1, 0, 2, 3, 4, 5).reshape(B, S, WIDTH_B)

def hybrid_mixer(x, w_in, q_gain, k_gain, sink, out_gain_a, out_gain_b, w_out, ang1d, ang2d):
    B, S = x.shape[0], x.shape[1]
    h = x @ w_in
    o1 = WIDTH_A
    o2 = o1 + KVW_A
    o3 = o2 + KVW_A
    o4 = o3 + WIDTH_B
    o5 = o4 + KVW_B
    qa, ka, va, qb, kb, vb = jnp.split(h, [o1, o2, o3, o4, o5], axis=-1)
    oa = global_axial_attention(qa.reshape(B, S, N_HEADS_A, HEAD_DIM), ka.reshape(B, S, N_KV_A, HEAD_DIM),
                                va.reshape(B, S, N_KV_A, HEAD_DIM), q_gain, k_gain, ang2d)
    ob = window_sink_attention(qb.reshape(B, S, N_HEADS_B, HEAD_DIM), kb.reshape(B, S, N_KV_B, HEAD_DIM),
                               vb.reshape(B, S, N_KV_B, HEAD_DIM), sink, ang1d)
    o = jnp.concatenate([rms_norm(oa, out_gain_a, NORM_EPS), rms_norm(ob, out_gain_b, NORM_EPS)], -1)
    return o.astype(x.dtype) @ w_out

def conv_glu(x, w_up, conv_w, conv_b, w_down):
    S = x.shape[1]
    g, v = jnp.split(x @ w_up, 2, axis=-1)
    gp = jnp.pad(g, ((0, 0), (1, 1), (0, 0)))
    g = gp[:, :S] * conv_w[0] + gp[:, 1:S + 1] * conv_w[1] + gp[:, 2:S + 2] * conv_w[2] + conv_b
    return (jax.nn.gelu(g) * v) @ w_down

def encoder_trunk(x, p, ln0_g, ln0_b, w_in, q_norm, k_norm, sink, out_norm_a, out_norm_b, w_out,
                  ln1_g, ln1_b, w_up, conv_w, conv_b, w_down, ln2_g, ln2_b, w_ple, w_ple_gate, b_ple_gate):
    S = x.shape[1]
    ang1d = rope_angles_1d(S)
    ang2d = rope_angles_2d(S)
    x = layer_norm(x, ln0_g, ln0_b)
    for i in range(DEPTH):
        mix = hybrid_mixer(x, w_in[i], q_norm[i], k_norm[i], sink[i], out_norm_a[i], out_norm_b[i],
                           w_out[i], ang1d, ang2d)
        x = layer_norm(ALPHA * x + mix, ln1_g[i], ln1_b[i])
        ffn = conv_glu(x, w_up[i], conv_w[i], conv_b[i], w_down[i])
        gate = jax.nn.sigmoid(x @ w_ple_gate[i] + b_ple_gate[i])
        ple = p[i].astype(x.dtype) @ w_ple[i]
        x = layer_norm(ALPHA * x + ffn + gate * ple, ln2_g[i], ln2_b[i])
    return x

def setup_inputs(seed: int = 0) -> dict:
    key = jax.random.key(seed)
    ks = jax.random.split(key, 24)
    nrm = lambda k, shp, s: jax.random.normal(k, shp, F32) * s
    return {
        'x_prompt': nrm(ks[0], (BATCH, SEQ, D_MODEL), 1.0),
        'x_sample': nrm(ks[1], (DEC_BATCH, DEC_SEQ, D_MODEL), 1.0),
        'p_prompt': nrm(ks[2], (DEPTH, BATCH, SEQ, D_PLE), 1.0),
        'p_sample': nrm(ks[3], (DEPTH, DEC_BATCH, DEC_SEQ, D_PLE), 1.0),
        'ln0_g': 1.0 + nrm(ks[4], (D_MODEL,), 0.02),
        'ln0_b': nrm(ks[5], (D_MODEL,), 0.02),
        'w_in': nrm(ks[6], (DEPTH, D_MODEL, IN_WIDTH), D_MODEL ** -0.5),
        'q_norm': 1.0 + nrm(ks[7], (DEPTH, HEAD_DIM), 0.02),
        'k_norm': 1.0 + nrm(ks[8], (DEPTH, HEAD_DIM), 0.02),
        'sink': nrm(ks[9], (DEPTH, N_HEADS_B), 1.0),
        'out_norm_a': 1.0 + nrm(ks[10], (DEPTH, WIDTH_A), 0.02),
        'out_norm_b': 1.0 + nrm(ks[11], (DEPTH, WIDTH_B), 0.02),
        'w_out': nrm(ks[12], (DEPTH, MIX_WIDTH, D_MODEL), BETA * MIX_WIDTH ** -0.5),
        'ln1_g': 1.0 + nrm(ks[13], (DEPTH, D_MODEL), 0.02),
        'ln1_b': nrm(ks[14], (DEPTH, D_MODEL), 0.02),
        'w_up': nrm(ks[15], (DEPTH, D_MODEL, 2 * D_FF), D_MODEL ** -0.5),
        'conv_w': nrm(ks[16], (DEPTH, CONV_W, D_FF), CONV_W ** -0.5),
        'conv_b': nrm(ks[17], (DEPTH, D_FF), 0.01),
        'w_down': nrm(ks[18], (DEPTH, D_FF, D_MODEL), BETA * D_FF ** -0.5),
        'ln2_g': 1.0 + nrm(ks[19], (DEPTH, D_MODEL), 0.02),
        'ln2_b': nrm(ks[20], (DEPTH, D_MODEL), 0.02),
        'w_ple': nrm(ks[21], (DEPTH, D_PLE, D_MODEL), BETA * D_PLE ** -0.5),
        'w_ple_gate': nrm(ks[22], (DEPTH, D_MODEL, D_MODEL), D_MODEL ** -0.5),
        'b_ple_gate': nrm(ks[23], (DEPTH, D_MODEL), 0.01),
    }

def reference(x_prompt, x_sample, p_prompt, p_sample, ln0_g, ln0_b, w_in, q_norm, k_norm, sink,
              out_norm_a, out_norm_b, w_out, ln1_g, ln1_b, w_up, conv_w, conv_b, w_down,
              ln2_g, ln2_b, w_ple, w_ple_gate, b_ple_gate):
    y_prompt = encoder_trunk(x_prompt, p_prompt, ln0_g, ln0_b, w_in, q_norm, k_norm, sink, out_norm_a,
                             out_norm_b, w_out, ln1_g, ln1_b, w_up, conv_w, conv_b, w_down, ln2_g, ln2_b,
                             w_ple, w_ple_gate, b_ple_gate)
    y_sample = encoder_trunk(x_sample, p_sample, ln0_g, ln0_b, w_in, q_norm, k_norm, sink, out_norm_a,
                             out_norm_b, w_out, ln1_g, ln1_b, w_up, conv_w, conv_b, w_down, ln2_g, ln2_b,
                             w_ple, w_ple_gate, b_ple_gate)
    return (y_prompt, y_sample)


_drawn_inputs = setup_inputs


def setup_inputs(seed=0):
    import zlib

    import numpy as np

    out = dict(_drawn_inputs(seed))
    spreads = {}
    factors = {'q_norm': 8.0,
     'k_norm': 8.0,
     'sink': 8.0,
     'out_norm_a': 6.965,
     'out_norm_b': 7.031,
     'conv_b': 8.0,
     'b_ple_gate': 8.0}
    for name, (base, spread) in spreads.items():
        noise = np.random.default_rng([zlib.crc32(name.encode()), seed]).standard_normal(out[name].shape)
        drawn = base * np.exp(spread * noise) if base else spread * noise
        out[name] = __import__('jax').numpy.asarray(drawn.astype(out[name].dtype))
    for name, factor in factors.items():
        out[name] = (out[name] * factor).astype(out[name].dtype)
    return out
```

```python
from contextlib import ExitStack

import concourse.bass as bass
import numpy as np
from concourse import mybir

F32 = mybir.dt.float32
F32R = mybir.dt.float32r
BF16 = mybir.dt.bfloat16
ALU = mybir.AluOpType
ACT = mybir.ActivationFunctionType
AX_X = mybir.AxisListType.X

P = 128
DEPTH = 2
D = 1024
SEQ = 256
TOK = 2 * SEQ
TT = TOK // P
KD = D // P
HD = 64
HEADS = 8
KV = 2
IN_W = 1536
FF = 2816
FT = FF // P
PLE = 256
KP = PLE // P
WINDOW = 128
GRID_W = 64
THETA = 10000.0
LN_EPS = 1e-5
QK_EPS = 1e-6
ALPHA = (2 * DEPTH) ** 0.25
MASKED = -1e30

SLOTS = 8
RAW = 2
IN_AT = 0
OUT_AT = 12
GATE_AT = 20
UP_AT = 30
DOWN_AT = UP_AT + 2 * FT
STREAM = DOWN_AT + FT
AHEAD = 4
LOOPED = 16
REST = FT - LOOPED
GROUPS = 4 * HEADS
COLS = 2 * 4 + 3 * FT + FT
assert STREAM % SLOTS == 0 and LOOPED % 4 == 0


def pe_plan():
    steps = []
    chunks = [(c, t) for c in range(2) for t in range(TT)]
    for i, (c, t) in enumerate(chunks):
        steps.append(("win", c, t))
        if i < 2:
            steps.append(("norm_in", i + 2))
        if i >= 1:
            steps.append(("rot", *chunks[i - 1]))
    for g in range(GROUPS + 2):
        if g < GROUPS:
            steps.append(("scores", g))
            steps.append(("win_part", g) if g < 16 else ("outa_part", g - 16))
        if 1 <= g <= GROUPS:
            steps.append(("probs_t", g - 1))
        if g >= 2:
            steps.append(("pv", g - 2))
        if g == 1:
            steps.append(("rot", 1, 3))
        if g in (6, 10, 14, 18):
            steps.append(("rot", 2, (g - 6) // 4))
        if g in (13, 21, 29):
            n = (g - 13) // 8
            steps += [("heads_t", n // 2, n % 2, 0), ("heads_t", n // 2, n % 2, 1)]
    steps += [("outb", 0), ("outb", 1), ("heads_t", 1, 1, 0), ("heads_t", 1, 1, 1), ("outb", 2), ("norm1", 0),
              ("outb", 3), ("norm1", 1), ("p_t",), ("gate", 0, 0), ("norm1", 2), ("gate", 0, 1), ("norm1", 3)]
    steps += [("gate", 0, 2), ("gate", 0, 3)] + [("gate", 1, t) for t in range(TT)]
    return steps


def transposes_of(steps):
    use, n = {}, 0
    for s in steps + [("norm2", 0), ("norm2", 1)]:
        if s[0] in ("rot", "probs_t", "heads_t"):
            use[s] = n
            n += 1
        if s[0] in ("norm_in", "norm1", "norm2"):
            use[s] = n
            n += 2
    return use, n


class Signal:

    def __init__(self, ctx, nc, name, per_layer, before=0):
        self.sem = ctx.enter_context(nc.semaphore(name))
        self.per_layer, self.before = per_layer, before

    def at(self, layer, n):
        return layer * self.per_layer + n + self.before


def encoder(nc, x_prompt, x_sample, p_prompt, p_sample, ln0_g, ln0_b, w_in, q_norm, k_norm, sink, columns,
            w_out, ln1_g, ln1_b, w_up, w_down, ln2_g, ln2_b, w_ple, w_ple_gate, b_ple_gate, rope, y_prompt, y_sample):
    STEPS = pe_plan()
    TR, TR_LAYER = transposes_of(STEPS)
    TR_BEFORE = 4
    assert TR_LAYER % 2 == 0

    with ExitStack() as ctx:
        def sb(name, shape, dt=F32):
            return ctx.enter_context(nc.sbuf_tensor(name, shape, dt))

        def sig(name, per_layer, before=0):
            return Signal(ctx, nc, name, per_layer, before)

        x = sb("x", [P, TT, D])
        xt_hi = sb("xt_hi", [P, KD, TOK], F32R)
        xt_lo = sb("xt_lo", [P, KD, TOK], F32R)
        s_hi = sb("s_hi", [P, 8, TOK], F32R)
        s_lo = sb("s_lo", [P, 8, TOK], F32R)
        w_hi = sb("w_hi", [P, SLOTS, 1024], F32R)
        w_lo = sb("w_lo", [P, SLOTS, 1024], F32R)
        raw = sb("raw", [P, RAW, 1024])
        hbuf = sb("hbuf", [P, LOOPED, TOK])
        qkt = hbuf[:, 0:12, :]
        vbuf = hbuf[:, 12:14, :].rearrange("p a (t n) -> p a t n", t=TT)
        rot = hbuf[:, 14:16, :]
        scratch = sb("scratch", [P, 6, 512])
        t1, t2 = scratch[:, 0, :], scratch[:, 1, :]
        squares = scratch[:, 2:4, :]
        probs = scratch[:, 2:4, :]
        probs_t = scratch[:, 4:6, :]
        ln_g = scratch[:, 0:2, :].rearrange("p a n -> p (a n)")
        ln_b = scratch[:, 2:4, :].rearrange("p a n -> p (a n)")
        gate_b = scratch[:, 4:6, :]
        heads_o = sb("heads_o", [P, 2, 512])
        p_in = heads_o[:, :, :].rearrange("p a (t n) -> p (a t) n", t=2)
        rope_sb = sb("rope_sb", [P, 4, 2, HD])
        rope_a = sb("rope_a", [P, 4, 2, HD])
        gains = heads_o[:, 0, 0:2 * HD].rearrange("p (a d) -> p a d", a=2)
        sinks = sb("sinks", [P, HEADS])
        neg_sinks = sb("neg_sinks", [P, HEADS])
        cols = sb("cols", [P, COLS])
        gain_o = cols[:, 0:8]
        conv_w = cols[:, 8:8 + 3 * FT].rearrange("p (a j) -> p a j", a=3)
        conv_b = cols[:, 8 + 3 * FT:]
        ident = sb("ident", [P, P])
        ident_b = sb("ident_b", [P, P], BF16)
        mask = sb("mask", [P, P], BF16)
        unused = sb("unused", [P, 512], BF16)
        bn = sb("bn", [P, 2, 6])
        mv = sb("mv", [P, TT, 2])
        ln_r = sb("ln_r", [P, TT])
        half_neg = sb("half_neg", [P, 8])
        ln_eps = sb("ln_eps", [P, 1])
        rqk = sb("rqk", [P, 2, TT, 8])
        row_max = sb("row_max", [P, 2, 2])
        neg_max = sb("neg_max", [P, 2, 2, 2, HEADS])
        den = sb("den", [P, 2, 2, 2, HEADS])
        sink_e = sb("sink_e", [P, 2, HEADS])
        oss = sb("oss", [P, 2])
        ps = ctx.enter_context(nc.psum_tensor("ps", [P, 8, 512], F32))
        SC, TRB, OB = 2, 4, 6
        DOWN_BANK = (4, 6, 0, 2)

        raw_landed = [sig(f"raw_landed{b}", 16 * STREAM // RAW, 16 * AHEAD // RAW) for b in range(RAW)]
        w_hi_done = sig("w_hi_done", STREAM, AHEAD)
        w_split = sig("w_split", STREAM, AHEAD)
        w_used = sig("w_used", STREAM, SLOTS)
        x_landed = [sig(f"x_landed{t}", 0) for t in range(TT)]
        fixed_landed = sig("fixed_landed", 0)
        const_landed = sig("const_landed", 16 * 4)
        norm_landed = sig("norm_landed", 16 * 4, 32)
        bias_landed = sig("bias_landed", 16)
        p_landed = sig("p_landed", 32)
        y_stored = sig("y_stored", 0)
        const_made = sig("const_made", 0)
        xt_split = sig("xt_split", 16, 4)
        xt_hi_done = sig("xt_hi_done", 16, 4)
        tr_full = sig("tr_full", TR_LAYER, TR_BEFORE)
        ln_var = sig("ln_var", 8, 4)
        ln_rstd = sig("ln_rstd", 8, 4)
        ln_done = sig("ln_done", 8, 4)
        win_full = sig("win_full", 9)
        win_act = sig("win_act", 12)
        win_free = sig("win_free", 12)
        qk_ss = sig("qk_ss", 8)
        qk_rstd = sig("qk_rstd", 8)
        rot_done = sig("rot_done", 12)
        qkt_done = sig("qkt_done", 12)
        sc_full = sig("sc_full", GROUPS)
        max_done = sig("max_done", GROUPS)
        exp_done = sig("exp_done", GROUPS)
        pt_dve = sig("pt_dve", GROUPS // 2)
        pt_act = sig("pt_act", GROUPS // 2)
        pv_done = sig("pv_done", GROUPS)
        sink_in = sig("sink_in", 2)
        sink_exp = sig("sink_exp", 2)
        o_evac = sig("o_evac", 8)
        o_ss = sig("o_ss", 8)
        o_rstd = sig("o_rstd", 8)
        o_norm = sig("o_norm", 8)
        ot_hi = sig("ot_hi", 8)
        ot_split = sig("ot_split", 8)
        outa_full = sig("outa_full", 6)
        outa_free = sig("outa_free", 8)
        outb_full = sig("outb_full", 3)
        outb_free = sig("outb_free", 4)
        p_full = sig("p_full", 1)
        p_hi = sig("p_hi", 1)
        p_split = sig("p_split", 1)
        gate_full = sig("gate_full", 6)
        gate_in = sig("gate_in", 8)
        gate_tanh = sig("gate_tanh", 8)
        gate_free = sig("gate_free", 8)
        ffn_begun = sig("ffn_begun", 1)
        gelu_begun = sig("gelu_begun", FT)
        conv_mid = sig("conv_mid", FT)
        conv_done = sig("conv_done", FT)
        gelu_done = sig("gelu_done", FT)
        h_done = sig("h_done", FT, 2)
        h_rest_hi = sig("h_rest_hi", REST)
        h_rest_split = sig("h_rest_split", REST)
        h_hi = sig("h_hi", LOOPED)
        h_split = sig("h_split", LOOPED)
        down_full = sig("down_full", 3)
        down_free = sig("down_free", 4, 4)

        block = ctx.enter_context(nc.Block())

        def slot(s, k=2):
            n = s % SLOTS
            return (w_hi[:, n, :].rearrange("p (k n) -> p k n", k=k),
                    w_lo[:, n, :].rearrange("p (k n) -> p k n", k=k))

        def wait_product(eng, layer, full, n, slots, last):
            if last:
                eng.wait_ge(w_used.sem, w_used.at(layer, slots))
            else:
                eng.wait_ge(full.sem, full.at(layer, n))

        def wait_win(eng, layer, c, t):
            wait_product(eng, layer, win_full, 3 * c + t + 1, IN_AT + 4 * c + 4, t == TT - 1)

        def wait_outa(eng, layer, t, n):
            wait_product(eng, layer, outa_full, 2 * t + n + 1, OUT_AT + 2 * n + 2, t == TT - 1)

        def wait_outb(eng, layer, t):
            wait_product(eng, layer, outb_full, t + 1, OUT_AT + 8, t == TT - 1)

        def wait_gate(eng, layer, n, t):
            wait_product(eng, layer, gate_full, 3 * n + t + 1, GATE_AT + 5 * n + 5, t == TT - 1)

        def wait_down(eng, layer, t):
            wait_product(eng, layer, down_full, t + 1, STREAM, t == TT - 1)

        def wait_up(eng, layer, value, j):
            eng.wait_ge(w_used.sem, w_used.at(layer, UP_AT + value + 1) + j * 2)

        def group(g):
            return g // 16, g // 8 % 2, g % 8

        @block.sync
        def _(sp):
            win_v = w_in.rearrange("l (q k p) n -> l q p k n", k=2, p=P)
            wout_v = w_out.rearrange("l (q k p) n -> l q p k n", k=2, p=P)
            gate_v = w_ple_gate.rearrange("l (q k p) n -> l q p k n", k=2, p=P)
            ple_v = w_ple.rearrange("l (k p) n -> l p k n", p=P)
            up_v = w_up.rearrange("l (k p) n -> l p k n", p=P)
            down_v = w_down.rearrange("l (j p) n -> (l j) p n", p=P)

            def load(s, src, k):
                b = s % RAW
                sp.dma_start(raw[:, b, :].rearrange("p (k n) -> p k n", k=k), src).then_inc(raw_landed[b].sem, 16)

            def one(ap):
                return ap.rearrange("a p k n -> (a p) k n")

            def source(s, layer):
                if s < OUT_AT:
                    c, q = divmod(s, 4)
                    return one(win_v[bass.ds(layer, 1), q, :, :, c * 512:(c + 1) * 512])
                if s < GATE_AT:
                    half, n, q = (s - OUT_AT) // 4, (s - OUT_AT) // 2 % 2, s % 2
                    return one(wout_v[bass.ds(layer, 1), half * 2 + q, :, :, n * 512:(n + 1) * 512])
                n, q = divmod(s - GATE_AT, 5)
                v = gate_v[bass.ds(layer, 1), q] if q < 4 else ple_v[bass.ds(layer, 1)]
                return one(v[:, :, :, n * 512:(n + 1) * 512])

            def up_source(layer, j, value):
                return one(up_v[bass.ds(layer, 1), :, :, bass.ds(j * P + value * FF, P)])

            def down_source(layer, j):
                return down_v[bass.ds(layer * FT + j, 1), :, :].rearrange("a p n -> p a n")

            def bcast(v):
                return v.partition_broadcast(P)

            for t in range(TT):
                src = (x_prompt, x_sample)[t // 2]
                sp.dma_start(x[:, t, :], src[0, t % 2 * P:(t % 2 + 1) * P, :]).then_inc(x_landed[t].sem, 16)
                if t == 0:
                    sp.dma_start(ln_g, bcast(ln0_g)).then_inc(norm_landed.sem, 16)
                    sp.dma_start(ln_b, bcast(ln0_b)).then_inc(norm_landed.sem, 16)
            for s in range(AHEAD):
                if s >= RAW:
                    sp.wait_ge(w_split.sem, s - RAW + 1)
                load(s, source(s, 0), 2)
            sp.dma_start(rope_sb[:, :, :, :], rope).then_inc(fixed_landed.sem, 16)

            with sp.Fori(0, DEPTH) as layer:
                def raw_free(s):
                    sp.wait_ge(w_split.sem, w_split.at(layer, s - AHEAD - RAW + 1))

                sp.wait_ge(h_done.sem, h_done.at(layer, 0))
                sp.dma_start(cols[:, :], columns[bass.ds(layer, 1)].rearrange("a p n -> (a p) n")).then_inc(const_landed.sem, 16)
                for i, v in enumerate((q_norm, k_norm)):
                    sp.dma_start(gains[:, i, :], bcast(v[bass.ds(layer, 1)].rearrange("a n -> (a n)"))).then_inc(const_landed.sem, 16)
                sp.dma_start(sinks[:, :], bcast(sink[bass.ds(layer, 1)].rearrange("a n -> (a n)"))).then_inc(const_landed.sem, 16)
                for s in range(AHEAD, UP_AT):
                    if s == 22:
                        sp.wait_ge(pv_done.sem, pv_done.at(layer, GROUPS))
                        sp.dma_start(ln_g, bcast(ln1_g[bass.ds(layer, 1)].rearrange("a n -> (a n)"))).then_inc(norm_landed.sem, 16)
                        sp.dma_start(ln_b, bcast(ln1_b[bass.ds(layer, 1)].rearrange("a n -> (a n)"))).then_inc(norm_landed.sem, 16)
                        sp.dma_start(gate_b.rearrange("p a n -> p (a n)"),
                                     bcast(b_ple_gate[bass.ds(layer, 1)].rearrange("a n -> (a n)"))).then_inc(bias_landed.sem, 16)
                    if s == 24:
                        sp.wait_ge(tr_full.sem, tr_full.at(layer, TR["heads_t", 1, 1, 1] + 1))
                        for i, v in enumerate((p_prompt, p_sample)):
                            sp.dma_start(p_in[:, 2 * i:2 * i + 2, :],
                                         v[bass.ds(layer, 1), 0].rearrange("a (t p) n -> p (a t) n", p=P)).then_inc(p_landed.sem, 16)
                    raw_free(s)
                    load(s, source(s, layer), 2)
                sp.wait_ge(ln_done.sem, ln_done.at(layer, 4))
                sp.dma_start(ln_g, bcast(ln2_g[bass.ds(layer, 1)].rearrange("a n -> (a n)"))).then_inc(norm_landed.sem, 16)
                sp.dma_start(ln_b, bcast(ln2_b[bass.ds(layer, 1)].rearrange("a n -> (a n)"))).then_inc(norm_landed.sem, 16)
                with sp.Fori(0, FT // 2) as i:
                    for v in range(4):
                        sp.wait_ge(w_split.sem, w_split.at(layer, UP_AT + v - AHEAD - RAW + 1) + i * 4)
                        load(UP_AT + v, up_source(layer, i * 2 + v // 2, v % 2), 8)
                raw_free(DOWN_AT)
                load(DOWN_AT, down_source(layer, LOOPED), 1)
                with sp.Fori(0, LOOPED // 2) as i:
                    for v in range(2):
                        s = DOWN_AT + 1 + v
                        sp.wait_ge(w_split.sem, w_split.at(layer, s - AHEAD - RAW + 1) + i * 2)
                        load(s, down_source(layer, i * 2 + v), 1)
                for r in range(1, REST):
                    raw_free(DOWN_AT + LOOPED + r)
                    load(DOWN_AT + LOOPED + r, down_source(layer, LOOPED + r), 1)
                following = (layer + 1) % DEPTH
                for s in range(AHEAD):
                    raw_free(STREAM + s)
                    load(s, source(s, following), 2)
            for t in range(TT):
                sp.wait_ge(ln_done.sem, ln_done.at(DEPTH - 1, 4 + t + 1))
                dst = (y_prompt, y_sample)[t // 2]
                sp.dma_start(dst[0, t % 2 * P:(t % 2 + 1) * P, :], x[:, t, :]).then_inc(y_stored.sem, 16)
            sp.wait_ge(y_stored.sem, 16 * TT)
            for b in range(RAW):
                sp.wait_ge(raw_landed[b].sem, raw_landed[b].at(DEPTH, 0))

        @block.gpsimd
        def _(pool):
            pool.memset(ident[:, :], 0.0)
            pool.memset(ident_b[:, :], 0.0)
            pool.memset(mask[:, :], 0.0)
            pool.memset(half_neg[:, :], -0.5)
            pool.memset(ln_eps[:, :], LN_EPS)
            pool.drain()
            pool.affine_select(out=ident[:, :], in_=ident[:, :], compare_op=ALU.not_equal, fill=1.0,
                               base=0, pattern=[[-1, P]], channel_multiplier=1)
            pool.affine_select(out=ident_b[:, :], in_=ident_b[:, :], compare_op=ALU.not_equal, fill=1.0,
                               base=0, pattern=[[-1, P]], channel_multiplier=1)
            pool.affine_select(out=mask[:, :], in_=mask[:, :], compare_op=ALU.is_ge, fill=MASKED,
                               base=0, pattern=[[-1, P]], channel_multiplier=1)
            pool.drain().then_inc(const_made.sem, 1)

            def lo(n, value):
                pool.wait_ge(w_hi_done.sem, value)
                pool.tensor_tensor(w_lo[:, n, :], raw[:, n % RAW, :], w_hi[:, n, :].bitcast(F32),
                                   ALU.subtract).then_inc(w_split.sem, 1)

            def ln_root(t, value):
                pool.wait_ge(ln_var.sem, value)
                pool.tensor_tensor(ln_r[:, t:t + 1], mv[:, t, 1:2], half_neg[:, 0:1], ALU.pow).then_inc(ln_rstd.sem, 1)

            for t in range(TT):
                ln_root(t, t + 1)
                lo(t, t + 1)

            with pool.Fori(0, DEPTH) as layer:
                def body_lo(s):
                    lo(s % SLOTS, w_hi_done.at(layer, s - AHEAD + 1))

                def o_root(kind, s):
                    for qt in range(2):
                        n = kind * 4 + s * 2 + qt
                        pool.wait_ge(o_ss.sem, o_ss.at(layer, n + 1))
                        pool.tensor_tensor(oss[:, qt:qt + 1], oss[:, qt:qt + 1], ln_eps[:, :], ALU.add)
                        pool.drain()
                        pool.tensor_tensor(oss[:, qt:qt + 1], oss[:, qt:qt + 1], half_neg[:, 0:1],
                                           ALU.pow).then_inc(o_rstd.sem, 1)

                for c in range(2):
                    for t in range(TT):
                        n = c * TT + t
                        w = (HEADS, KV)[c]
                        pool.wait_ge(qk_ss.sem, qk_ss.at(layer, n + 1))
                        pool.tensor_tensor(rqk[:, c, t, 0:w], rqk[:, c, t, 0:w], half_neg[:, 0:w],
                                           ALU.pow).then_inc(qk_rstd.sem, 1)
                        body_lo(4 + n)
                for g in range(GROUPS + 2):
                    if g in (2, 5, 8, 11):
                        body_lo(12 + (g - 2) // 3)
                    if g in (17, 18, 19, 20):
                        body_lo(16 + g - 17)
                    if g in (10, 18, 26):
                        o_root((g - 10) // 8 // 2, (g - 10) // 8 % 2)
                o_root(1, 1)
                for s in (20, 21, 22, 23):
                    body_lo(s)
                    ln_root(s - 20, ln_var.at(layer, s - 20 + 1))
                for s in range(24, 38):
                    body_lo(s)
                with pool.Fori(0, LOOPED // 4) as i:
                    for v in range(8):
                        lo((38 + v) % SLOTS, w_hi_done.at(layer, 38 + v - AHEAD + 1) + i * 8)
                for s in range(38 + 2 * LOOPED, DOWN_AT + 6):
                    body_lo(s)
                with pool.Fori(0, LOOPED // 8) as i:
                    for v in range(8):
                        lo((DOWN_AT + 6 + v) % SLOTS, w_hi_done.at(layer, DOWN_AT + 6 + v - AHEAD + 1) + i * 8)
                body_lo(STREAM)
                body_lo(STREAM + 1)
                ln_root(0, ln_var.at(layer, 5))
                ln_root(1, ln_var.at(layer, 6))
                ln_root(2, ln_var.at(layer, 7))
                body_lo(STREAM + 2)
                body_lo(STREAM + 3)
                ln_root(3, ln_var.at(layer, 8))

        @block.scalar
        def _(act):
            def hi(n, landed, used):
                act.wait_ge(raw_landed[n % RAW].sem, landed)
                act.wait_ge(w_used.sem, used)
                act.activation(w_hi[:, n, :], raw[:, n % RAW, :], ACT.Copy).then_inc(w_hi_done.sem, 1)

            def norm_hi(t, full):
                for b in range(2):
                    act.wait_ge(tr_full.sem, full + b)
                    act.activation(xt_hi[:, 4 * b:4 * b + 4, t * P:(t + 1) * P],
                                   ps[:, TRB + b, :].rearrange("p (k n) -> p k n", k=4), ACT.Copy).then_inc(xt_hi_done.sem, 1)

            for s in range(AHEAD):
                hi(s, 16 * (s // RAW + 1), s + 1)
            for t in range(2):
                norm_hi(t, 2 * t + 1)

            with act.Fori(0, DEPTH) as layer:
                def body_hi(s):
                    hi(s % SLOTS, raw_landed[s % RAW].at(layer, 16 * ((s - AHEAD) // RAW + 1)), w_used.at(layer, s - SLOTS + 1))

                def looped_hi(s, i):
                    hi(s % SLOTS, raw_landed[s % RAW].at(layer, 16 * ((s - AHEAD) // RAW + 1)) + i * (16 * 8 // RAW),
                       w_used.at(layer, s - SLOTS + 1) + i * 8)

                def win(c, t):
                    n = c * TT + t
                    bank = ps[:, n % 2, :]
                    wait_win(act, layer, c, t)
                    if c == 0:
                        act.wait_ge(ln_done.sem, ln_done.at(layer, 0))
                        if n >= 2:
                            act.wait_ge(qk_ss.sem, qk_ss.at(layer, n - 1))
                        act.activation(squares[:, n % 2, :], bank, ACT.Square).then_inc(win_act.sem, 1)
                    elif c == 1:
                        act.wait_ge(qk_ss.sem, qk_ss.at(layer, n - 1))
                        act.activation(vbuf[:, 0, t, :], bank[:, 128:256], ACT.Copy)
                        act.activation(squares[:, n % 2, 0:128], bank[:, 0:128], ACT.Square).then_inc(win_act.sem, 1)
                    else:
                        act.activation(vbuf[:, 1, t, :], bank[:, 384:512], ACT.Copy).then_inc(win_act.sem, 1)

                def qkt_evac(c, t):
                    u = TR["rot", c, t]
                    act.wait_ge(tr_full.sem, tr_full.at(layer, u + 1))
                    ins = act.activation(qkt[:, 4 * c:4 * c + 4, t * P:(t + 1) * P],
                                         ps[:, TRB + u % 2, :].rearrange("p (k n) -> p k n", k=4), ACT.Copy)
                    ins.then_inc(qkt_done.sem, 1)

                def exps(g):
                    kind, s, h = group(g)
                    act.wait_ge(max_done.sem, max_done.at(layer, g + 1))
                    if g >= 2:
                        act.wait_ge(tr_full.sem, tr_full.at(layer, TR["probs_t", g - 2] + 1))
                    for qt in range(2):
                        scale = 0.125 if kind else rqk[:, 0, 2 * s + qt, h:h + 1]
                        ins = act.activation(probs[:, g % 2, qt * 256:(qt + 1) * 256],
                                             ps[:, SC + g % 2, qt * 256:(qt + 1) * 256], ACT.Exp,
                                             bias=neg_max[:, kind, s, qt, h:h + 1], scale=scale,
                                             accum_out=den[:, kind, s, qt, h:h + 1])
                    ins.then_inc(exp_done.sem, 1)

                def probs_evac(g):
                    u = TR["probs_t", g]
                    act.wait_ge(tr_full.sem, tr_full.at(layer, u + 1))
                    if g >= 2:
                        act.wait_ge(pv_done.sem, pv_done.at(layer, g - 1))
                    act.activation(probs_t[:, g % 2, :], ps[:, TRB + u % 2, :], ACT.Copy).then_inc(pt_act.sem, 1)

                def o_squares(kind, s):
                    for qt in range(2):
                        if qt:
                            act.drain()
                        act.wait_ge(o_evac.sem, o_evac.at(layer, kind * 4 + s * 2 + qt + 1))
                        act.activation(unused[:, :], heads_o[:, qt, :], ACT.Square, scale=512 ** -0.5,
                                       accum_out=oss[:, qt:qt + 1]).then_inc(o_ss.sem, 1)

                def heads_hi(kind, s):
                    for qt in range(2):
                        u = TR["heads_t", kind, s, qt]
                        t = 2 * s + qt
                        act.wait_ge(tr_full.sem, tr_full.at(layer, u + 1))
                        for k in range(4):
                            ins = act.activation(s_hi[:, 4 * kind + k, t * P:(t + 1) * P],
                                                 ps[:, TRB + u % 2, k * P:(k + 1) * P], ACT.Copy,
                                                 scale=gain_o[:, 4 * kind + k:4 * kind + k + 1])
                        ins.then_inc(ot_hi.sem, 1)

                def gate(n, t):
                    q = n * TT + t
                    act.wait_ge(gate_in.sem, gate_in.at(layer, q + 1))
                    act.activation(heads_o[:, q % 2, :], heads_o[:, q % 2, :], ACT.Tanh, scale=0.5).then_inc(gate_tanh.sem, 1)

                def conv_centre(bank, j, dst, n):
                    wait_up(act, layer, 0, n)
                    act.activation(dst, ps[:, bank, :], ACT.Identity, bias=conv_b[:, bass.ds(j, 1)],
                                   scale=conv_w[:, 1, bass.ds(j, 1)]).then_inc(conv_mid.sem, 1)

                def gelu(dst, n):
                    act.wait_ge(conv_done.sem, conv_done.at(layer, 1) + n)
                    act.sem_inc(gelu_begun.sem, 1)
                    act.activation(dst, dst, ACT.Gelu_apprx_tanh).then_inc(gelu_done.sem, 1)

                act.wait_ge(const_landed.sem, const_landed.at(layer, 64))
                for c in range(2):
                    for t in range(TT):
                        win(c, t)
                        if c == 0 and t < 2:
                            norm_hi(t + 2, tr_full.at(layer, TR["norm_in", t + 2] + 1))
                        if c or t:
                            qkt_evac(*divmod(c * TT + t - 1, TT))
                        body_hi(4 + c * TT + t)
                for g in range(GROUPS + 2):
                    if g < GROUPS:
                        exps(g)
                    if 1 <= g <= GROUPS and (g - 1) % 2:
                        probs_evac(g - 1)
                        
                    if g == 1:
                        qkt_evac(1, 3)
                    if g in (6, 10, 14, 18):
                        qkt_evac(2, (g - 6) // 4)
                    if g in (13, 21, 29):
                        heads_hi((g - 13) // 8 // 2, (g - 13) // 8 % 2)
                    if g in (3, 7, 11, 15):
                        win(2, (g - 3) // 4)
                    if g in (2, 5, 8, 11):
                        body_hi(12 + (g - 2) // 3)
                    if g in (17, 18, 19, 20):
                        body_hi(16 + g - 17)
                    if g in (25, 33):
                        n = (g - 25) // 8
                        act.wait_ge(sink_in.sem, sink_in.at(layer, n + 1))
                        act.activation(sink_e[:, :, :], sink_e[:, :, :], ACT.Exp).then_inc(sink_exp.sem, 1)
                    if g in (9, 17, 25, 33):
                        n = (g - 9) // 8
                        o_squares(n // 2, n % 2)
                body_hi(20)
                body_hi(21)
                heads_hi(1, 1)
                body_hi(22)
                norm_hi(0, tr_full.at(layer, TR["norm1", 0] + 1))
                body_hi(23)
                norm_hi(1, tr_full.at(layer, TR["norm1", 1] + 1))
                body_hi(24)
                act.wait_ge(p_full.sem, p_full.at(layer, 1))
                ins = act.activation(s_hi[:, 0:KP, :], ps[:, OB:OB + KP, :], ACT.Copy, scale=0.5)
                ins.then_inc(p_hi.sem, 1)
                norm_hi(2, tr_full.at(layer, TR["norm1", 2] + 1))
                gate(0, 0)
                body_hi(25)
                norm_hi(3, tr_full.at(layer, TR["norm1", 3] + 1))
                gate(0, 1)
                body_hi(26)
                gate(0, 2)
                body_hi(27)
                body_hi(28)
                gate(0, 3)
                body_hi(29)
                gate(1, 0)
                body_hi(30)
                body_hi(31)
                gate(1, 1)
                body_hi(32)
                gate(1, 2)
                body_hi(33)
                gate(1, 3)
                for s in range(34, 38):
                    body_hi(s)

                with act.Fori(0, LOOPED // 4) as i:
                    for v in range(4):
                        dst = hbuf[:, bass.ds(i * 4 + v, 1), :].rearrange("p a n -> p (a n)")
                        conv_centre(2 * (v % 2), i * 4 + v, dst, i * 4 + v)
                        looped_hi(38 + 2 * v, i)
                        gelu(dst, i * 4 + v)
                        looped_hi(39 + 2 * v, i)
                for r in range(REST):
                    j = LOOPED + r
                    dst = scratch[:, 4 + r % 2, :]
                    if r >= 2:
                        act.wait_ge(h_rest_split.sem, h_rest_split.at(layer, r - 1))
                    conv_centre(2 * (j % 2), j, dst, j)
                    if j < FT - 1:
                        body_hi(38 + 2 * j)
                    gelu(dst, j)
                    if j < FT - 1:
                        body_hi(39 + 2 * j)
                    act.wait_ge(h_done.sem, h_done.at(layer, j + 1))
                    act.activation(s_hi[:, r, :], dst, ACT.Copy).then_inc(h_rest_hi.sem, 1)
                with act.Fori(0, LOOPED // 8) as i:
                    for v in range(8):
                        act.wait_ge(w_used.sem, w_used.at(layer, DOWN_AT + v) + i * 8)
                        act.activation(s_hi[:, 6 + v % 2, :], hbuf[:, bass.ds(i * 8 + v, 1), :].rearrange("p a n -> p (a n)"),
                                       ACT.Copy).then_inc(h_hi.sem, 1)
                        looped_hi(DOWN_AT + 6 + v, i)
                body_hi(STREAM)
                body_hi(STREAM + 1)
                norm_hi(0, tr_full.at(layer, TR["norm2", 0] + 1))
                norm_hi(1, tr_full.at(layer, TR["norm2", 1] + 1))
                body_hi(STREAM + 2)
                body_hi(STREAM + 3)

        @block.vector
        def _(dve):
            def norm_stats(t):
                for b in range(2):
                    dve.bn_stats(bn[:, b, :], x[:, t, b * 512:(b + 1) * 512])
                dve.drain()
                dve.bn_aggr(mv[:, t, :], bn[:, :, :].rearrange("p a n -> p (a n)"))
                dve.drain()
                dve.tensor_scalar(mv[:, t, 1:2], mv[:, t, 1:2], LN_EPS, None, ALU.add).then_inc(ln_var.sem, 1)

            def norm_apply(t, rstd, landed):
                dve.wait_ge(norm_landed.sem, landed)
                dve.scalar_tensor_tensor(out=x[:, t, :], in0=x[:, t, :], scalar=mv[:, t, 0:1], in1=ln_g,
                                         op0=ALU.subtract, op1=ALU.mult)
                dve.drain()
                dve.wait_ge(ln_rstd.sem, rstd)
                dve.scalar_tensor_tensor(out=x[:, t, :], in0=x[:, t, :], scalar=ln_r[:, t:t + 1], in1=ln_b,
                                         op0=ALU.mult, op1=ALU.add).then_inc(ln_done.sem, 1)

            def norm_lo(t, hi):
                for b in range(2):
                    dve.wait_ge(xt_hi_done.sem, hi + b)
                    dve.tensor_tensor(xt_lo[:, 4 * b:4 * b + 4, t * P:(t + 1) * P],
                                      ps[:, TRB + b, :].rearrange("p (k n) -> p k n", k=4),
                                      xt_hi[:, 4 * b:4 * b + 4, t * P:(t + 1) * P].bitcast(F32),
                                      ALU.subtract).then_inc(xt_split.sem, 1)

            for t in range(TT):
                dve.wait_ge(x_landed[t].sem, 16)
                norm_stats(t)
                norm_apply(t, t + 1, 32)
            for t in range(2):
                norm_lo(t, 2 * t + 1)
            dve.wait_ge(fixed_landed.sem, 16)

            with dve.Fori(0, DEPTH) as layer:
                def turn(v, heads, bank_cols, cs, sn, t):
                    src = v.rearrange("p (h d) -> p h d", h=heads)
                    swapped = v.rearrange("p (h i b) -> p h i b", h=heads, b=2)[:, :, :, ::-1]
                    shape = [P, heads, HD]
                    a = t1[:, bank_cols].rearrange("p (h d) -> p h d", h=heads)
                    b = t2[:, bank_cols].rearrange("p (h i b) -> p h i b", h=heads, b=2)
                    dve.tensor_tensor(a, src, cs[:, t % 2, :].unsqueeze(1).to_broadcast(shape), ALU.mult)
                    return dve.tensor_tensor(b, swapped,
                                             sn[:, t % 2, :].rearrange("p (i b) -> p i b", b=2).unsqueeze(1)
                                             .to_broadcast([P, heads, HD // 2, 2]), ALU.mult)

                def rotate(c, t):
                    n = c * TT + t
                    bank = ps[:, n % 2, :]
                    out = rot[:, n % 2, :]
                    dve.wait_ge(win_act.sem, win_act.at(layer, n + 1))
                    if n >= 2:
                        c2, tt2 = divmod(n - 2, TT)
                        dve.wait_ge(tr_full.sem, tr_full.at(layer, TR["rot", c2, tt2] + 1))
                    if c < 2:
                        w = (HEADS, KV)[c]
                        dve.tensor_reduce(rqk[:, c, t, 0:w], squares[:, n % 2, 0:w * HD].rearrange("p (h d) -> p h d", h=w),
                                          AX_X, ALU.add)
                        dve.drain()
                        dve.tensor_scalar(rqk[:, c, t, 0:w], rqk[:, c, t, 0:w], HD * QK_EPS, None,
                                          ALU.add).then_inc(qk_ss.sem, 1)
                    if c == 0:
                        turn(bank, HEADS, slice(0, 512), rope_a[:, 0], rope_a[:, 1], t).then_inc(win_free.sem, 1)
                        dve.drain()
                        dve.tensor_tensor(out, t1, t2, ALU.add).then_inc(rot_done.sem, 1)
                    elif c == 1:
                        turn(bank[:, 0:128], KV, slice(0, 128), rope_a[:, 2], rope_a[:, 3], t)
                        turn(bank[:, 256:512], 4, slice(256, 512), rope_sb[:, 2], rope_sb[:, 3], t).then_inc(win_free.sem, 1)
                        dve.drain()
                        dve.tensor_tensor(out[:, 256:512], t1[:, 256:512], t2[:, 256:512], ALU.add)
                        dve.tensor_tensor(t1[:, 0:128], t1[:, 0:128], t2[:, 0:128], ALU.add)
                        dve.drain()
                        dve.wait_ge(qk_rstd.sem, qk_rstd.at(layer, n + 1))
                        shape = [P, KV, 2, HD]
                        dve.tensor_tensor(out[:, 0:256].rearrange("p (v e d) -> p v e d", v=KV, e=2),
                                          t1[:, 0:128].rearrange("p (v d) -> p v d", v=KV).unsqueeze(2).to_broadcast(shape),
                                          rqk[:, 1, t, 0:KV].unsqueeze(2).unsqueeze(3).to_broadcast(shape),
                                          ALU.mult).then_inc(rot_done.sem, 1)
                    else:
                        turn(bank[:, 0:384], 6, slice(0, 384), rope_sb[:, 2], rope_sb[:, 3], t).then_inc(win_free.sem, 1)
                        dve.drain()
                        dve.tensor_tensor(out[:, 0:256], t1[:, 0:256], t2[:, 0:256], ALU.add)
                        shape = [P, KV, 2, HD]
                        dve.tensor_tensor(out[:, 256:512].rearrange("p (v e d) -> p v e d", v=KV, e=2),
                                          t1[:, 256:384].rearrange("p (v d) -> p v d", v=KV).unsqueeze(2).to_broadcast(shape),
                                          t2[:, 256:384].rearrange("p (v d) -> p v d", v=KV).unsqueeze(2).to_broadcast(shape),
                                          ALU.add).then_inc(rot_done.sem, 1)

                def maxima(g):
                    kind, s, h = group(g)
                    mx = row_max[:, g % 2, :]
                    dve.wait_ge(sc_full.sem, sc_full.at(layer, g + 1))
                    dve.tensor_reduce(mx, ps[:, SC + g % 2, :].rearrange("p (q n) -> p q n", q=2), AX_X, ALU.max)
                    dve.drain()
                    if g == 0:
                        dve.wait_ge(qk_rstd.sem, qk_rstd.at(layer, 2 * TT))
                    if kind == 0:
                        dve.scalar_tensor_tensor(out=neg_max[:, 0, s, :, h], in0=mx, scalar=-1.0,
                                                 in1=rqk[:, 0, 2 * s:2 * s + 2, h], op0=ALU.mult,
                                                 op1=ALU.mult).then_inc(max_done.sem, 1)
                    else:
                        dve.tensor_scalar(neg_max[:, 1, s, :, h], mx, -0.125, neg_sinks[:, h:h + 1], ALU.mult,
                                          ALU.min).then_inc(max_done.sem, 1)

                def probs_evac(g):
                    u = TR["probs_t", g]
                    dve.wait_ge(tr_full.sem, tr_full.at(layer, u + 1))
                    if g >= 2:
                        dve.wait_ge(pv_done.sem, pv_done.at(layer, g - 1))
                    dve.tensor_copy(probs_t[:, g % 2, :], ps[:, TRB + u % 2, :]).then_inc(pt_dve.sem, 1)

                def heads_evac(kind, s):
                    n = kind * 2 + s
                    d = den[:, kind, s, :, :]
                    dve.wait_ge(exp_done.sem, exp_done.at(layer, 8 * n + 8))
                    if kind:
                        dve.tensor_tensor(sink_e[:, :, :], neg_max[:, 1, s, :, :],
                                          sinks[:, :].unsqueeze(1).to_broadcast([P, 2, HEADS]), ALU.add).then_inc(sink_in.sem, 1)
                        dve.wait_ge(sink_exp.sem, sink_exp.at(layer, s + 1))
                        dve.tensor_tensor(d, d, sink_e[:, :, :], ALU.add)
                        dve.drain()
                    dve.reciprocal(d, d)
                    dve.drain()
                    if n:
                        k2, s2 = divmod(n - 1, 2)
                        dve.wait_ge(tr_full.sem, tr_full.at(layer, TR["heads_t", k2, s2, 1] + 1))
                    dve.wait_ge(pv_done.sem, pv_done.at(layer, 8 * n + 8))
                    for qt in range(2):
                        dve.tensor_tensor(heads_o[:, qt, :].rearrange("p (h d) -> p h d", h=HEADS),
                                          ps[:, OB + qt, :].rearrange("p (h d) -> p h d", h=HEADS),
                                          den[:, kind, s, qt, :].unsqueeze(2).to_broadcast([P, HEADS, HD]),
                                          ALU.mult).then_inc(o_evac.sem, 1)

                def heads_norm(kind, s):
                    for qt in range(2):
                        dve.wait_ge(o_rstd.sem, o_rstd.at(layer, kind * 4 + s * 2 + qt + 1))
                        dve.tensor_scalar(heads_o[:, qt, :], heads_o[:, qt, :], oss[:, qt:qt + 1], None,
                                          ALU.mult).then_inc(o_norm.sem, 1)

                def heads_lo(kind, s):
                    for qt in range(2):
                        u = TR["heads_t", kind, s, qt]
                        t = 2 * s + qt
                        dve.wait_ge(ot_hi.sem, ot_hi.at(layer, kind * 4 + t + 1))
                        for k in range(4):
                            ins = dve.scalar_tensor_tensor(out=s_lo[:, 4 * kind + k, t * P:(t + 1) * P],
                                                           in0=ps[:, TRB + u % 2, k * P:(k + 1) * P],
                                                           scalar=gain_o[:, 4 * kind + k:4 * kind + k + 1],
                                                           in1=s_hi[:, 4 * kind + k, t * P:(t + 1) * P].bitcast(F32),
                                                           op0=ALU.mult, op1=ALU.subtract)
                        ins.then_inc(ot_split.sem, 1)

                def outa(t, n):
                    wait_outa(dve, layer, t, n)
                    xs = x[:, t, n * 512:(n + 1) * 512]
                    dve.scalar_tensor_tensor(out=xs, in0=xs, scalar=ALPHA, in1=ps[:, n, :], op0=ALU.mult,
                                             op1=ALU.add).then_inc(outa_free.sem, 1)

                def add_banks(t, bank, freed):
                    dve.tensor_tensor(x[:, t, :], x[:, t, :], ps[:, bank:bank + 2, :].rearrange("p a n -> p (a n)"),
                                      ALU.add).then_inc(freed.sem, 1)
                    dve.drain()

                def outb(t):
                    wait_outb(dve, layer, t)
                    add_banks(t, 2 * (t % 2), outb_free)
                    norm_stats(t)
                    norm_apply(t, ln_rstd.at(layer, t + 1), norm_landed.at(layer, 32))

                def gate_sum(n, t):
                    q = n * TT + t
                    wait_gate(dve, layer, n, t)
                    if q == 0:
                        dve.wait_ge(bias_landed.sem, bias_landed.at(layer, 16))
                    dve.tensor_tensor(heads_o[:, q % 2, :], ps[:, q % 2, :], gate_b[:, n, :], ALU.add).then_inc(gate_in.sem, 1)

                def gate_apply(n, t):
                    q = n * TT + t
                    buf = heads_o[:, q % 2, :]
                    dve.wait_ge(gate_tanh.sem, gate_tanh.at(layer, q + 1))
                    dve.scalar_tensor_tensor(out=buf, in0=buf, scalar=1.0, in1=ps[:, SC + q % 2, :], op0=ALU.add,
                                             op1=ALU.mult).then_inc(gate_free.sem, 1)
                    dve.drain()
                    xs = x[:, t, n * 512:(n + 1) * 512]
                    dve.scalar_tensor_tensor(out=xs, in0=xs, scalar=ALPHA, in1=buf, op0=ALU.mult, op1=ALU.add)

                def conv_sides(bank, j, dst, n):
                    dve.wait_ge(conv_mid.sem, conv_mid.at(layer, 1) + n)
                    d = dst.rearrange("p (s n) -> p s n", s=2)
                    g = ps[:, bank, :].rearrange("p (s n) -> p s n", s=2)
                    dve.scalar_tensor_tensor(out=d[:, :, 1:], in0=g[:, :, 0:SEQ - 1], scalar=conv_w[:, 0, bass.ds(j, 1)],
                                             in1=d[:, :, 1:], op0=ALU.mult, op1=ALU.add)
                    dve.drain()
                    dve.scalar_tensor_tensor(out=d[:, :, 0:SEQ - 1], in0=g[:, :, 1:], scalar=conv_w[:, 2, bass.ds(j, 1)],
                                             in1=d[:, :, 0:SEQ - 1], op0=ALU.mult, op1=ALU.add).then_inc(conv_done.sem, 1)

                def glu(bank, dst, n):
                    wait_up(dve, layer, 1, n)
                    dve.wait_ge(gelu_done.sem, gelu_done.at(layer, 1) + n)
                    dve.tensor_tensor(dst, dst, ps[:, bank + 1, :], ALU.mult).then_inc(h_done.sem, 1)

                dve.wait_ge(const_landed.sem, const_landed.at(layer, 64))
                for i in range(2):
                    g = gains[:, i, :].unsqueeze(1).to_broadcast([P, 2, HD])
                    gs = (gains[:, i, :].rearrange("p (i b) -> p i b", b=2)[:, :, ::-1].unsqueeze(1)
                          .to_broadcast([P, 2, HD // 2, 2]))
                    dve.tensor_tensor(rope_a[:, 2 * i, :, :], rope_sb[:, 0, :, :], g, ALU.mult)
                    dve.tensor_tensor(rope_a[:, 2 * i + 1, :, :].rearrange("p t (i b) -> p t i b", b=2),
                                      rope_sb[:, 1, :, :].rearrange("p t (i b) -> p t i b", b=2), gs, ALU.mult)
                dve.tensor_scalar(neg_sinks[:, :], sinks[:, :], -1.0, None, ALU.mult)
                dve.drain()
                dve.tensor_scalar(rope_a[:, 2:4, :, :], rope_a[:, 2:4, :, :], 8.0, None, ALU.mult)
                dve.drain()

                norm_lo(2, xt_hi_done.at(layer, 1))
                for c in range(2):
                    for t in range(TT):
                        rotate(c, t)
                        if c == 0 and t == 0:
                            norm_lo(3, xt_hi_done.at(layer, 3))
                for g in range(GROUPS + 2):
                    if g < GROUPS:
                        maxima(g)
                    if 1 <= g <= GROUPS and (g - 1) % 2 == 0:
                        probs_evac(g - 1)
                    if g in (4, 8, 12, 16):
                        rotate(2, (g - 4) // 4)
                    if g in (13, 21, 29):
                        heads_lo((g - 13) // 8 // 2, (g - 13) // 8 % 2)
                    if g in (9, 17, 25, 33):
                        n = (g - 9) // 8
                        heads_evac(n // 2, n % 2)
                    if g in (11, 19, 27):
                        n = (g - 11) // 8
                        heads_norm(n // 2, n % 2)
                    if 16 <= g < 32 and g % 2:
                        outa(*divmod((g - 16) // 2, 2))
                heads_norm(1, 1)
                outb(0)
                heads_lo(1, 1)
                outb(1)
                norm_lo(0, xt_hi_done.at(layer, 5))
                outb(2)
                norm_lo(1, xt_hi_done.at(layer, 7))
                outb(3)
                dve.wait_ge(p_hi.sem, p_hi.at(layer, 1))
                dve.scalar_tensor_tensor(out=s_lo[:, 0:KP, :], in0=ps[:, OB:OB + KP, :], scalar=0.5,
                                         in1=s_hi[:, 0:KP, :].bitcast(F32), op0=ALU.mult,
                                         op1=ALU.subtract).then_inc(p_split.sem, 1)
                norm_lo(2, xt_hi_done.at(layer, 9))
                for q in range(2 * TT):
                    gate_sum(*divmod(q, TT))
                    if q == 0:
                        norm_lo(3, xt_hi_done.at(layer, 11))
                    gate_apply(*divmod(q, TT))

                with dve.Fori(0, LOOPED // 4) as i:
                    for v in range(4):
                        dst = hbuf[:, bass.ds(i * 4 + v, 1), :].rearrange("p a n -> p (a n)")
                        conv_sides(2 * (v % 2), i * 4 + v, dst, i * 4 + v)
                        glu(2 * (v % 2), dst, i * 4 + v)
                for r in range(REST):
                    j = LOOPED + r
                    dst = scratch[:, 4 + r % 2, :]
                    conv_sides(2 * (j % 2), j, dst, j)
                    glu(2 * (j % 2), dst, j)
                    dve.wait_ge(h_rest_hi.sem, h_rest_hi.at(layer, r + 1))
                    dve.tensor_tensor(s_lo[:, r, :], dst, s_hi[:, r, :].bitcast(F32), ALU.subtract).then_inc(h_rest_split.sem, 1)
                with dve.Fori(0, LOOPED // 8) as i:
                    for v in range(8):
                        dve.wait_ge(h_hi.sem, h_hi.at(layer, v + 1) + i * 8)
                        dve.tensor_tensor(s_lo[:, 6 + v % 2, :], hbuf[:, bass.ds(i * 8 + v, 1), :].rearrange("p a n -> p (a n)"),
                                          s_hi[:, 6 + v % 2, :].bitcast(F32), ALU.subtract).then_inc(h_split.sem, 1)
                for t in range(TT):
                    wait_down(dve, layer, t)
                    add_banks(t, DOWN_BANK[t], down_free)
                    norm_stats(t)
                    norm_apply(t, ln_rstd.at(layer, 4 + t + 1), norm_landed.at(layer, 64))
                    if t in (1, 2):
                        norm_lo(t - 1, xt_hi_done.at(layer, 13 + 2 * (t - 1)))

        @block.tensor
        def _(pe):
            def product(out, a, b, first, last):
                pe.matmul(out, a[0], b[0], start=first, stop=False)
                pe.matmul(out, a[0], b[1], start=False, stop=False)
                return pe.matmul(out, a[1], b[0], start=False, stop=last)

            def norm_t(t, ready):
                pe.wait_ge(ln_done.sem, ready)
                for b in range(2):
                    yield b
                    for k in range(4):
                        ins = pe.transpose(ps[:, TRB + b, k * P:(k + 1) * P], x[:, t, (4 * b + k) * P:(4 * b + k + 1) * P],
                                           ident[:, :])
                    ins.then_inc(tr_full.sem, 1)

            def xt(k, t):
                return xt_hi[:, k, t * P:(t + 1) * P], xt_lo[:, k, t * P:(t + 1) * P]

            pe.sem_inc(w_used.sem, SLOTS)
            pe.sem_inc(h_done.sem, 2)
            pe.sem_inc(down_free.sem, 4)
            pe.wait_ge(const_made.sem, 1)
            for t in range(2):
                for b in norm_t(t, t + 1):
                    if t:
                        pe.wait_ge(xt_split.sem, b + 1)

            with pe.Fori(0, DEPTH) as layer:
                def split(s):
                    pe.wait_ge(w_split.sem, w_split.at(layer, s - AHEAD + 1))

                def body_norm_t(t, step, ready):
                    for b in norm_t(t, ready):
                        wait_bank(TR[step] + b)

                def wait_bank(u):
                    before = [s for s, n in TR.items() if n == u - 2 or (s[0].startswith("norm") and n == u - 3)]
                    if not before:
                        pe.wait_ge(xt_split.sem, xt_split.at(layer, u % 2 - 1))
                        return
                    s = before[0]
                    if s[0] == "norm_in":
                        pe.wait_ge(xt_split.sem, xt_split.at(layer, 2 * (s[1] - 2) + u - 2 - TR[s] + 1))
                    elif s[0] == "norm1":
                        pe.wait_ge(xt_split.sem, xt_split.at(layer, 4 + 2 * s[1] + u - 2 - TR[s] + 1))
                    elif s[0] == "norm2":
                        pe.wait_ge(xt_split.sem, xt_split.at(layer, 12 + 2 * s[1] + u - 2 - TR[s] + 1))
                    elif s[0] == "rot":
                        pe.wait_ge(qkt_done.sem, qkt_done.at(layer, s[1] * TT + s[2] + 1))
                    elif s[0] == "probs_t":
                        done = pt_act if s[1] % 2 else pt_dve
                        pe.wait_ge(done.sem, done.at(layer, s[1] // 2 + 1))
                    else:
                        pe.wait_ge(ot_split.sem, ot_split.at(layer, s[1] * 4 + s[2] * 2 + s[3] + 1))

                def win_quarter(c, t, q):
                    n = c * TT + t
                    if t == 0:
                        split(IN_AT + 4 * c + q)
                    if q == 0:
                        if c < 2:
                            pe.wait_ge(xt_split.sem, 16 * layer + 2 * t + 2)
                        if n >= 2:
                            pe.wait_ge(win_free.sem, win_free.at(layer, n - 1))
                        else:
                            pe.wait_ge(down_free.sem, down_free.at(layer, -1))
                    b = slot(IN_AT + 4 * c + q)
                    for k in range(2):
                        ins = product(ps[:, n % 2, :], xt(2 * q + k, t), (b[0][:, k, :], b[1][:, k, :]),
                                      q == 0 and k == 0, q == 3 and k == 1)
                    return ins

                def out_quarter(half, t, n, q, bank):
                    s = OUT_AT + 4 * half + 2 * n + q
                    if t == 0:
                        split(s)
                    b = slot(s)
                    for k in range(2):
                        kk = 4 * half + 2 * q + k
                        ins = product(ps[:, bank, :], (s_hi[:, kk, t * P:(t + 1) * P], s_lo[:, kk, t * P:(t + 1) * P]),
                                      (b[0][:, k, :], b[1][:, k, :]), q == 0 and k == 0, q == 1 and k == 1)
                    return ins

                def signal(ins, full, closes, t):
                    if t == TT - 1:
                        ins.then_inc(w_used.sem, 1)
                    elif closes:
                        ins.then_inc(full.sem, 1)

                for step in STEPS:
                    kind = step[0]
                    if kind == "win":
                        _, c, t = step
                        for q in range(4):
                            ins = win_quarter(c, t, q)
                            signal(ins, win_full, q == 3, t)
                    elif kind == "win_part":
                        t, q = divmod(step[1], 4)
                        ins = win_quarter(2, t, q)
                        signal(ins, win_full, q == 3, t)
                    elif kind == "norm_in":
                        body_norm_t(step[1], step, ln_done.at(layer, step[1] - 3))
                    elif kind == "rot":
                        _, c, t = step
                        u = TR[step]
                        pe.wait_ge(rot_done.sem, rot_done.at(layer, c * TT + t + 1))
                        wait_bank(u)
                        for k in range(4):
                            ins = pe.transpose(ps[:, TRB + u % 2, k * P:(k + 1) * P], rot[:, t % 2, k * P:(k + 1) * P], ident[:, :])
                        ins.then_inc(tr_full.sem, 1)
                    elif kind == "scores":
                        g = step[1]
                        k, s, h = group(g)
                        if g < 2:
                            pe.wait_ge(down_free.sem, down_free.at(layer, 0))
                        else:
                            pe.wait_ge(exp_done.sem, exp_done.at(layer, g - 1))
                        if g % 8 == 0:
                            pe.wait_ge(qkt_done.sem, qkt_done.at(layer, TT * (1 + k) + 2 * s + 2))
                        pair = h // 2 + (6 if k else 0)
                        key = h // 4 + (10 if k else 4)
                        rows = slice(HD * (h % 2), HD * (h % 2) + HD)
                        for qt in range(2):
                            t = 2 * s + qt
                            out = ps[:, SC + g % 2, qt * 256:(qt + 1) * 256]
                            ins = pe.matmul(out, qkt[rows, pair, t * P:(t + 1) * P], qkt[rows, key, s * SEQ:(s + 1) * SEQ],
                                            start=True, stop=(k == 0), skip_group_check=True)
                            if k:
                                a, b = (mask, ident_b) if qt else (ident_b, mask)
                                ins = pe.matmul(out[:, (1 - qt) * P:(2 - qt) * P], a[:, :], b[:, :],
                                                start=False, stop=True, skip_group_check=True)
                        ins.then_inc(sc_full.sem, 1)
                    elif kind == "probs_t":
                        g = step[1]
                        u = TR[step]
                        pe.wait_ge(exp_done.sem, exp_done.at(layer, g + 1))
                        wait_bank(u)
                        for kb in range(2):
                            for qt in range(2):
                                ins = pe.transpose(ps[:, TRB + u % 2, kb * 256 + qt * P:kb * 256 + (qt + 1) * P],
                                                   probs[:, g % 2, qt * 256 + kb * P:qt * 256 + (kb + 1) * P], ident[:, :])
                        ins.then_inc(tr_full.sem, 1)
                    elif kind == "pv":
                        g = step[1]
                        k, s, h = group(g)
                        done = pt_act if g % 2 else pt_dve
                        pe.wait_ge(done.sem, done.at(layer, g // 2 + 1))
                        if g == 0:
                            pe.wait_ge(down_free.sem, down_free.at(layer, -2))
                        elif h == 0:
                            pe.wait_ge(o_evac.sem, o_evac.at(layer, g // 4))
                        for qt in range(2):
                            for kb in range(2):
                                ins = pe.matmul(ps[:, OB + qt, h * HD:(h + 1) * HD],
                                                probs_t[:, g % 2, kb * 256 + qt * P:kb * 256 + (qt + 1) * P],
                                                vbuf[:, k, 2 * s + kb, h // 4 * HD:(h // 4 + 1) * HD],
                                                start=(kb == 0), stop=(kb == 1))
                        ins.then_inc(pv_done.sem, 1)
                    elif kind == "heads_t":
                        _, k, s, qt = step
                        u = TR[step]
                        pe.wait_ge(o_norm.sem, o_norm.at(layer, k * 4 + s * 2 + qt + 1))
                        wait_bank(u)
                        for b in range(4):
                            ins = pe.transpose(ps[:, TRB + u % 2, b * P:(b + 1) * P], heads_o[:, qt, b * P:(b + 1) * P], ident[:, :])
                        ins.then_inc(tr_full.sem, 1)
                    elif kind == "outa_part":
                        t, r = divmod(step[1], 4)
                        n, q = divmod(r, 2)
                        if r == 0:
                            pe.wait_ge(ot_split.sem, ot_split.at(layer, t + 1))
                        if q == 0:
                            if t == 0:
                                pe.wait_ge(win_free.sem, win_free.at(layer, 11 + n))
                            else:
                                pe.wait_ge(outa_free.sem, outa_free.at(layer, 2 * t + n - 1))
                        ins = out_quarter(0, t, n, q, n)
                        signal(ins, outa_full, q == 1, t)
                    elif kind == "outb":
                        t = step[1]
                        pe.wait_ge(ot_split.sem, ot_split.at(layer, 4 + t + 1))
                        if t == 0:
                            pe.wait_ge(outa_free.sem, outa_free.at(layer, 8))
                        elif t == 1:
                            pe.wait_ge(exp_done.sem, exp_done.at(layer, GROUPS))
                        else:
                            pe.wait_ge(outb_free.sem, outb_free.at(layer, t - 1))
                        for n in range(2):
                            for q in range(2):
                                ins = out_quarter(1, t, n, q, 2 * (t % 2) + n)
                                signal(ins, outb_full, n and q, t)
                    elif kind == "norm1":
                        body_norm_t(step[1], step, ln_done.at(layer, step[1] + 1))
                    elif kind == "p_t":
                        pe.wait_ge(p_landed.sem, p_landed.at(layer, 32))
                        pe.wait_ge(o_evac.sem, o_evac.at(layer, 8))
                        for k in range(KP):
                            for t in range(TT):
                                ins = pe.transpose(ps[:, OB + k, t * P:(t + 1) * P], p_in[:, t, k * P:(k + 1) * P], ident[:, :])
                        ins.then_inc(p_full.sem, 1)
                    elif kind == "gate":
                        _, n, t = step
                        i = n * TT + t
                        if n == 0:
                            pe.wait_ge(xt_split.sem, xt_split.at(layer, 4 + 2 * t + 2))
                        if i < 2:
                            pe.wait_ge(outb_free.sem, outb_free.at(layer, 4))
                        else:
                            pe.wait_ge(gate_free.sem, gate_free.at(layer, i - 1))
                        base = GATE_AT + 5 * n
                        for q in range(4):
                            if t == 0:
                                split(base + q)
                            b = slot(base + q)
                            for k in range(2):
                                ins = product(ps[:, i % 2, :], xt(2 * q + k, t), (b[0][:, k, :], b[1][:, k, :]),
                                              q == 0 and k == 0, q == 3 and k == 1)
                            signal(ins, None, False, t)
                        if i == 0:
                            pe.wait_ge(p_split.sem, p_split.at(layer, 1))
                        if t == 0:
                            split(base + 4)
                        b = slot(base + 4)
                        for k in range(KP):
                            ins = product(ps[:, SC + i % 2, :], (s_hi[:, k, t * P:(t + 1) * P], s_lo[:, k, t * P:(t + 1) * P]),
                                          (b[0][:, k, :], b[1][:, k, :]), k == 0, k == KP - 1)
                        signal(ins, gate_full, True, t)

                def up_tile(bank, s, n):
                    pe.wait_ge(h_done.sem, h_done.at(layer, -1) + n)
                    for v in range(2):
                        pe.wait_ge(w_split.sem, w_split.at(layer, s[0] + v - AHEAD + 1) + s[1])
                        a = slot(s[0] + v, KD)
                        for k in range(KD):
                            ins = product(ps[:, bank + v, :], (a[0][:, k, :], a[1][:, k, :]), (xt_hi[:, k, :], xt_lo[:, k, :]),
                                          k == 0, k == KD - 1)
                        ins.then_inc(w_used.sem, 1)

                pe.wait_ge(gate_free.sem, gate_free.at(layer, 8))
                pe.wait_ge(xt_split.sem, xt_split.at(layer, 12))
                pe.sem_inc(ffn_begun.sem, 1)
                with pe.Fori(0, LOOPED // 4) as i:
                    for v in range(4):
                        up_tile(2 * (v % 2), (UP_AT + 2 * v, i * 8), i * 4 + v)
                for j in range(LOOPED, FT):
                    up_tile(2 * (j % 2), (UP_AT + 2 * j, 0), j)

                def down(j, s, t, first, last):
                    b = slot(s, 1)
                    for n in range(2):
                        ins = product(ps[:, DOWN_BANK[t] + n, :], (s_hi[:, j, t * P:(t + 1) * P], s_lo[:, j, t * P:(t + 1) * P]),
                                      (b[0][:, 0, n * 512:(n + 1) * 512], b[1][:, 0, n * 512:(n + 1) * 512]), first, last)
                    return ins

                split(DOWN_AT)
                pe.wait_ge(h_rest_split.sem, h_rest_split.at(layer, 1))
                for t in range(TT):
                    if t >= 2:
                        pe.wait_ge(h_done.sem, h_done.at(layer, FT - 3 + t))
                    ins = down(0, DOWN_AT, t, True, False)
                ins.then_inc(w_used.sem, 1)
                with pe.Fori(0, LOOPED // 8) as i:
                    for v in range(8):
                        s = DOWN_AT + 1 + v
                        pe.wait_ge(h_split.sem, h_split.at(layer, v + 1) + i * 8)
                        pe.wait_ge(w_split.sem, w_split.at(layer, s - AHEAD + 1) + i * 8)
                        for t in range(TT):
                            ins = down(6 + v % 2, s, t, False, False)
                        ins.then_inc(w_used.sem, 1)
                pe.wait_ge(h_rest_split.sem, h_rest_split.at(layer, REST))
                for t in range(TT):
                    for r in range(1, REST):
                        if t == 0:
                            split(DOWN_AT + LOOPED + r)
                        ins = down(r, DOWN_AT + LOOPED + r, t, False, r == REST - 1)
                        signal(ins, down_full, r == REST - 1, t)
                    if t in (1, 2):
                        if t == 1:
                            pe.wait_ge(down_free.sem, down_free.at(layer, 1))
                        body_norm_t(t - 1, ("norm2", t - 1), ln_done.at(layer, 4 + t))


def _rope():
    pos = np.arange(SEQ, dtype=np.float32)

    def inverse(width):
        return np.float32(THETA) ** (-np.arange(0, width, 2, dtype=np.float32) / np.float32(width))

    inv2 = inverse(HD // 2)
    row, col = np.floor(pos / GRID_W).astype(np.float32), (pos % GRID_W).astype(np.float32)
    axial = np.concatenate([row[:, None] * inv2[None], col[:, None] * inv2[None]], -1)
    plain = pos[:, None] * inverse(HD)[None]
    tables = []
    for angle in (axial, plain):
        c, s = np.cos(angle), np.sin(angle)
        tables += [np.repeat(c, 2, -1), np.stack([-s, s], -1).reshape(SEQ, HD)]
    t = np.stack(tables).astype(np.float32).reshape(4, SEQ // P, P, HD)
    return np.ascontiguousarray(t.transpose(2, 0, 1, 3))


def _columns(a):
    return a.reshape(DEPTH, -1, P).transpose(0, 2, 1)


def kernel(**inputs):
    import concourse.bacc as bacc
    from concourse.bass_utils import run_bass_kernel_spmd

    nc = bacc.Bacc("TRN2", target_bir_lowering=False, num_devices=1)
    arrays, args = {}, []

    def add(name, a):
        a = np.ascontiguousarray(a)
        arrays[f"in_{name}_dram"] = a
        args.append(nc.dram_tensor(f"in_{name}_dram", a.shape, mybir.dt.from_np(a.dtype), kind="ExternalInput").ap())

    given = {k: np.asarray(v) for k, v in inputs.items()}
    for name in ("x_prompt", "x_sample", "p_prompt", "p_sample", "ln0_g", "ln0_b", "w_in", "q_norm", "k_norm", "sink"):
        add(name, given[name])
    conv = given["conv_w"].reshape(DEPTH, 3, FT, P).transpose(0, 3, 1, 2).reshape(DEPTH, P, 3 * FT)
    add("columns", np.concatenate([_columns(given["out_norm_a"]), _columns(given["out_norm_b"]), conv,
                                   _columns(given["conv_b"])], -1))
    for name in ("w_out", "ln1_g", "ln1_b", "w_up", "w_down", "ln2_g", "ln2_b", "w_ple", "w_ple_gate", "b_ple_gate"):
        add(name, given[name])
    add("rope", _rope())
    for name in ("y_prompt", "y_sample"):
        args.append(nc.dram_tensor(f"out_{name}_dram", (1, SEQ, D), F32, kind="ExternalOutput").ap())
    encoder(nc, *args)
    r = run_bass_kernel_spmd(nc, [arrays], core_ids=[0])
    return tuple(r.results[0][f"out_{name}_dram"] for name in ("y_prompt", "y_sample"))
```

```python
from contextlib import ExitStack

import concourse.bass as bass
import numpy as np
from concourse import mybir

F32 = mybir.dt.float32
F32R = mybir.dt.float32r
BF16 = mybir.dt.bfloat16
ALU = mybir.AluOpType
ACT = mybir.ActivationFunctionType
AX_X = mybir.AxisListType.X

P = 128
DEPTH = 2
D = 1024
SEQ = 256
TOK = 2 * SEQ
TT = TOK // P
KD = D // P
HD = 64
HEADS = 8
KV = 2
IN_W = 1536
FF = 2816
FT = FF // P
PLE = 256
KP = PLE // P
WINDOW = 128
GRID_W = 64
THETA = 10000.0
LN_EPS = 1e-5
QK_EPS = 1e-6
ALPHA = (2 * DEPTH) ** 0.25
MASKED = -1e30

WARM = (8, 9)
SLOTS = 8
RAW = 2
IN_AT = 0
OUT_AT = 12
PLE_AT = 16
OUTB_AT = 18
GATE_AT = 22
UP_AT = 30
DOWN_AT = UP_AT + 2 * FT
STREAM = DOWN_AT + FT
AHEAD = 4
LOOPED = 16
REST = FT - LOOPED
GROUPS = 4 * HEADS
COLS = 3 * FT + FT
assert STREAM % SLOTS == 0 and LOOPED % 4 == 0


def pe_plan():
    steps = []
    for n in range(2 * TT):
        c, t = divmod(n, TT)
        steps.append(("win", c, t, 0))
        if n == 2:
            steps.append(("rot", 0, 0))
        steps.append(("win", c, t, 1))
        if n < 2:
            steps.append(("norm_in", n + 2))
        else:
            steps.append(("rot", *divmod(n - 1, TT)))
    for g in range(GROUPS + 3):
        if g < GROUPS:
            steps.append(("scores", g))
            if g < 2:
                steps += [("win_part", 2 * g), ("win_part", 2 * g + 1)]
            elif g < 14:
                steps.append(("win_part", g + 2))
            elif g > 15:
                steps.append(("outa_part", g - 16))
        if 2 <= g < GROUPS + 2:
            steps.append(("probs_t", g - 2))
        if g >= GROUPS:
            steps.append(("ple", 0, g - GROUPS))
        if g >= 3:
            steps.append(("pv", g - 3))
        if g == 1:
            steps.append(("rot", 1, 3))
        if g in (5, 9, 13, 17):
            steps.append(("rot", 2, (g - 5) // 4))
        if g in (14, 15, 22, 23, 30, 31):
            steps.append(("heads_t", (g - 14) // 16, (g - 14) // 8 % 2, g % 2))
        if g in (28, 29):
            steps.append(("p_t", g - 28))
    steps += [("ple", 0, 3), ("outb", 0), ("heads_t", 1, 1, 0), ("heads_t", 1, 1, 1), *[("ple", 1, t) for t in range(TT)], ("outb", 1),
              ("outb", 2), ("norm1", 0), ("outb", 3), ("norm1", 1), ("gate", 0, 0), ("norm1", 2), ("gate", 0, 1),
              ("norm1", 3)]
    steps += [("gate", 0, 2), ("gate", 0, 3)] + [("gate", 1, t) for t in range(TT)]
    return steps


def transposes_of(steps):
    use, n = {}, 0
    for s in steps + [("norm2", 0), ("norm2", 1)]:
        if s[0] in ("rot", "probs_t", "heads_t", "p_t"):
            use[s] = n
            n += 1
        if s[0] in ("norm_in", "norm1", "norm2"):
            use[s] = n
            n += 2
    return use, n


class Signal:

    def __init__(self, ctx, nc, name, per_layer, before=0):
        self.sem = ctx.enter_context(nc.semaphore(name))
        self.per_layer, self.before = per_layer, before

    def at(self, layer, n):
        return layer * self.per_layer + n + self.before


def encoder(nc, x_prompt, x_sample, p_prompt, p_sample, ln0_g, ln0_b, w_in, q_norm, k_norm, sink, out_norm_a,
            out_norm_b, columns,
            w_out, ln1_g, ln1_b, w_up, w_down, ln2_g, ln2_b, w_ple, w_ple_gate, b_ple_gate, rope, y_prompt, y_sample):
    STEPS = pe_plan()
    TR, TR_LAYER = transposes_of(STEPS)
    TR_BEFORE = 4
    assert TR_LAYER % 2 == 0

    with ExitStack() as ctx:
        def sb(name, shape, dt=F32):
            return ctx.enter_context(nc.sbuf_tensor(name, shape, dt))

        def sig(name, per_layer, before=0):
            return Signal(ctx, nc, name, per_layer, before)

        x = sb("x", [P, TT, D])
        xt_hi = sb("xt_hi", [P, KD, TOK], F32R)
        xt_lo = sb("xt_lo", [P, KD, TOK], F32R)
        stat = sb("stat", [P, 2, 8, TOK], F32R)
        s_hi, s_lo = stat[:, 0], stat[:, 1]
        w_hi = sb("w_hi", [P, SLOTS, 1024], F32R)
        w_lo = sb("w_lo", [P, SLOTS, 1024], F32R)
        raw = sb("raw", [P, RAW, 1024])
        with nc.sbuf_tensor("k_split", [P, 8, TOK], F32R) as k_split:
            pass
        hbuf = sb("hbuf", [P, LOOPED, TOK])
        o_gain = hbuf[:, 8:10, :]
        vbuf = hbuf[:, 12:14, :].rearrange("p a (t n) -> p a t n", t=TT)
        rot = hbuf[:, 14:16, :]
        p_in = rot.rearrange("p a (t n) -> p (a t) n", t=2)
        ple = hbuf[:, 0:8, :]
        scratch = sb("scratch", [P, 6, 512])
        t1, t2 = scratch[:, 0, :], scratch[:, 1, :]
        squares = scratch[:, 2:4, :]
        probs = scratch[:, 2:4, :]
        probs_t = scratch[:, 4:6, :]
        ln_g = scratch[:, 0:2, :].rearrange("p a n -> p (a n)")
        ln_b = scratch[:, 2:4, :].rearrange("p a n -> p (a n)")
        gate_b = scratch[:, 4:6, :]
        heads_o = sb("heads_o", [P, 2, 512])
        rope_sb = sb("rope_sb", [P, 4, 2, HD])
        rope_a = sb("rope_a", [P, 4, 2, HD])
        gains = heads_o[:, 0, 0:2 * HD].rearrange("p (a d) -> p a d", a=2)
        sinks = sb("sinks", [P, HEADS])
        neg_sinks = sb("neg_sinks", [P, HEADS])
        cols = sb("cols", [P, COLS])
        conv_w = cols[:, 0:3 * FT].rearrange("p (a j) -> p a j", a=3)
        conv_b = cols[:, 3 * FT:]
        ident = sb("ident", [P, P])
        ident_b = sb("ident_b", [P, P], BF16)
        mask = sb("mask", [P, P], BF16)
        unused = sb("unused", [P, 512], BF16)
        bn = sb("bn", [P, 2, 6])
        mv = sb("mv", [P, TT, 2])
        ln_r = sb("ln_r", [P, TT])
        half_neg = sb("half_neg", [P, 8])
        ln_eps = sb("ln_eps", [P, 1])
        rqk = sb("rqk", [P, 2, TT, 8])
        row_max = sb("row_max", [P, 2, 2])
        neg_max = sb("neg_max", [P, 2, 2, 2, HEADS])
        den = sb("den", [P, 2, 2, 2, HEADS])
        sink_e = sb("sink_e", [P, 2, HEADS])
        oss = sb("oss", [P, 2])
        ps = ctx.enter_context(nc.psum_tensor("ps", [P, 8, 512], F32))
        SC, TRB, OB = 2, 4, 6
        OUTB_BANK = (0, 6, 2, 0)
        DOWN_BANK = (4, 6, 0, 2)

        raw_landed = [sig(f"raw_landed{b}", 16 * STREAM // RAW, 16) for b in range(RAW)]
        stage_landed = [sig(f"stage_landed{b}", 0) for b in range(AHEAD - RAW)]
        w_hi_done = sig("w_hi_done", STREAM, AHEAD)
        w_split = sig("w_split", STREAM, AHEAD)
        w_used = sig("w_used", STREAM, SLOTS)
        x_landed = [sig(f"x_landed{t}", 0) for t in range(TT)]
        fixed_landed = sig("fixed_landed", 0)
        const_landed = sig("const_landed", 16 * 4)
        o_gain_landed = sig("o_gain_landed", 32)
        first_gain_landed = sig("first_gain_landed", 0)
        norm_landed = sig("norm_landed", 16 * 4, 16)
        bias_landed = sig("bias_landed", 16)
        p_landed = sig("p_landed", 32)
        y_stored = sig("y_stored", 0)
        const_made = sig("const_made", 0)
        xt_split = sig("xt_split", 16, 4)
        xt_hi_done = sig("xt_hi_done", 16, 4)
        tr_full = sig("tr_full", TR_LAYER, TR_BEFORE)
        ln_var = sig("ln_var", 8, 4)
        ln_rstd = sig("ln_rstd", 8, 4)
        ln_done = sig("ln_done", 8, 4)
        ln_half = sig("ln_half", 1)
        win_full = sig("win_full", 9)
        win_act = sig("win_act", 12)
        win_free = sig("win_free", 12)
        qk_ss = sig("qk_ss", 8)
        qk_rstd = sig("qk_rstd", 8)
        rot_done = sig("rot_done", 12)
        qkt_hi = sig("qkt_hi", 12)
        qkt_done = sig("qkt_done", 12)
        sc_full = sig("sc_full", GROUPS)
        max_done = sig("max_done", GROUPS)
        exp_done = sig("exp_done", GROUPS)
        pt_dve = sig("pt_dve", GROUPS // 2)
        pt_act = sig("pt_act", GROUPS // 2)
        pv_done = sig("pv_done", GROUPS)
        sink_in = sig("sink_in", 2)
        sink_exp = sig("sink_exp", 2)
        o_evac = sig("o_evac", 8)
        o_ss = sig("o_ss", 8)
        o_rstd = sig("o_rstd", 8)
        o_norm = sig("o_norm", 8)
        ot_hi = sig("ot_hi", 8)
        ot_split = sig("ot_split", 8)
        outa_full = sig("outa_full", 6)
        outa_free = sig("outa_free", 8)
        outb_full = sig("outb_full", 3)
        outb_free = sig("outb_free", 4)
        p_hi = sig("p_hi", KP)
        p_split = sig("p_split", KP)
        ple_full = sig("ple_full", 6)
        ple_free = sig("ple_free", 8)
        gate_full = sig("gate_full", 6)
        gate_in = sig("gate_in", 8)
        gate_tanh = sig("gate_tanh", 8)
        ffn_begun = sig("ffn_begun", 1)
        gelu_begun = sig("gelu_begun", FT)
        conv_mid = sig("conv_mid", FT)
        conv_done = sig("conv_done", FT)
        gelu_done = sig("gelu_done", FT)
        h_done = sig("h_done", FT, 2)
        h_rest_hi = sig("h_rest_hi", REST)
        h_rest_split = sig("h_rest_split", REST)
        h_hi = sig("h_hi", LOOPED)
        h_split = sig("h_split", LOOPED)
        down_full = sig("down_full", 4)
        down_free = sig("down_free", 4, 4)

        block = ctx.enter_context(nc.Block())

        def first_raw(s):
            return raw[:, s, :] if s < RAW else hbuf[:, 2 * (s - RAW):2 * (s - RAW) + 2, :].rearrange("p a n -> p (a n)")

        def slot(s, k=2):
            n = s % SLOTS
            return (w_hi[:, n, :].rearrange("p (k n) -> p k n", k=k),
                    w_lo[:, n, :].rearrange("p (k n) -> p k n", k=k))

        def wait_product(eng, layer, full, n, slots, last):
            if last:
                eng.wait_ge(w_used.sem, w_used.at(layer, slots))
            else:
                eng.wait_ge(full.sem, full.at(layer, n))

        def wait_win(eng, layer, c, t):
            wait_product(eng, layer, win_full, 3 * c + t + 1, IN_AT + 4 * c + 4, t == TT - 1)

        def wait_outa(eng, layer, t, n):
            wait_product(eng, layer, outa_full, 2 * t + n + 1, OUT_AT + 2 * n + 2, t == TT - 1)

        def wait_outb(eng, layer, t):
            wait_product(eng, layer, outb_full, t + 1, OUTB_AT + 4, t == TT - 1)

        def wait_gate(eng, layer, n, t):
            wait_product(eng, layer, gate_full, 3 * n + t + 1, GATE_AT + 4 * n + 4, t == TT - 1)

        def wait_ple(eng, layer, n, t):
            wait_product(eng, layer, ple_full, 3 * n + t + 1, PLE_AT + n + 1, t == TT - 1)

        def wait_down(eng, layer, t):
            wait_product(eng, layer, down_full, t + 1, STREAM, t == TT - 1)

        def wait_up(eng, layer, value, j):
            eng.wait_ge(w_used.sem, w_used.at(layer, UP_AT + value + 1) + j * 2)

        def q_stack(kind, h):
            return h // 4, 4 * kind + h % 4

        def k_block(kind, v, lo):
            return 4 * kind + 2 * lo + v

        def q_parts(c, u, odd):
            rows = slice(HD * odd, HD * odd + HD)
            bank = ps[rows, TRB + u % 2, :]
            if c == 0:
                return bank.rearrange("p (a b n) -> p a b n", a=2, b=2), slice(0, 2), slice(odd, 4, 2)
            at = 256 if c == 1 else 0
            return (bank[:, at:at + 256].rearrange("p (a b n) -> p a b n", a=1, b=2), slice(c - 1, c),
                    slice(4 + odd, 8, 2))

        def k_parts(c, u):
            at = 0 if c == 1 else 256
            first = 4 * (c - 1)
            return (ps[:, TRB + u % 2, at:at + 256].rearrange("p (v n) -> p v n", v=KV), slice(first, first + 2),
                    slice(first + 2, first + 4))

        def group(g):
            return g // 16, g // 8 % 2, g % 8

        @block.sync
        def _(sp):
            win_v = w_in.rearrange("l (q k p) n -> l q p k n", k=2, p=P)
            wout_v = w_out.rearrange("l (q k p) n -> l q p k n", k=2, p=P)
            gate_v = w_ple_gate.rearrange("l (q k p) n -> l q p k n", k=2, p=P)
            ple_v = w_ple.rearrange("l (k p) n -> l p k n", p=P)
            up_v = w_up.rearrange("l (k p) n -> l p k n", p=P)
            down_v = w_down.rearrange("l (j p) n -> (l j) p n", p=P)

            def load(s, src, k):
                b = s % RAW
                sp.dma_start(raw[:, b, :].rearrange("p (k n) -> p k n", k=k), src).then_inc(raw_landed[b].sem, 16)

            def one(ap):
                return ap.rearrange("a p k n -> (a p) k n")

            def source(s, layer):
                if s < OUT_AT:
                    c, q = divmod(s, 4)
                    return one(win_v[bass.ds(layer, 1), q, :, :, c * 512:(c + 1) * 512])
                if PLE_AT <= s < OUTB_AT:
                    n = s - PLE_AT
                    return one(ple_v[bass.ds(layer, 1), :, :, n * 512:(n + 1) * 512])
                if s < GATE_AT:
                    half = s >= OUTB_AT
                    n, q = divmod(s - (OUTB_AT if half else OUT_AT), 2)
                    return one(wout_v[bass.ds(layer, 1), half * 2 + q, :, :, n * 512:(n + 1) * 512])
                n, q = divmod(s - GATE_AT, 4)
                return one(gate_v[bass.ds(layer, 1), q, :, :, n * 512:(n + 1) * 512])

            def up_source(layer, j, value):
                return one(up_v[bass.ds(layer, 1), :, :, bass.ds(j * P + value * FF, P)])

            def down_source(layer, j):
                return down_v[bass.ds(layer * FT + j, 1), :, :].rearrange("a p n -> p a n")

            def bcast(v):
                return v.partition_broadcast(P)

            def load_x(t):
                src = (x_prompt, x_sample)[t // 2]
                sp.dma_start(x[:, t, :], src[0, t % 2 * P:(t % 2 + 1) * P, :]).then_inc(x_landed[t].sem, 16)

            load_x(0)
            sp.dma_start(ln_g, bcast(ln0_g)).then_inc(first_gain_landed.sem, 16)
            sp.dma_start(ln_b, bcast(ln0_b)).then_inc(norm_landed.sem, 16)
            load_x(1)
            def first_load(s):
                landed = raw_landed[s] if s < RAW else stage_landed[s - RAW]
                sp.dma_start(first_raw(s).rearrange("p (k n) -> p k n", k=2), source(s, 0)).then_inc(landed.sem, 16)

            first_load(0)
            first_load(1)
            first_load(2)
            load_x(2)
            first_load(3)
            load_x(3)
            sp.dma_start(rope_sb[:, :, :, :], rope).then_inc(fixed_landed.sem, 16)

            with sp.Fori(0, DEPTH) as layer:
                def raw_free(s):
                    sp.wait_ge(w_split.sem, w_split.at(layer, s - AHEAD - RAW + 1))

                sp.wait_ge(h_done.sem, h_done.at(layer, 0))
                sp.dma_start(cols[:, :], columns[bass.ds(layer, 1)].rearrange("a p n -> (a p) n")).then_inc(const_landed.sem, 16)
                for i, v in enumerate((q_norm, k_norm)):
                    sp.dma_start(gains[:, i, :], bcast(v[bass.ds(layer, 1)].rearrange("a n -> (a n)"))).then_inc(const_landed.sem, 16)
                sp.dma_start(sinks[:, :], bcast(sink[bass.ds(layer, 1)].rearrange("a n -> (a n)"))).then_inc(const_landed.sem, 16)
                for s in range(AHEAD, UP_AT):
                    if s == 24:
                        sp.wait_ge(pv_done.sem, pv_done.at(layer, GROUPS))
                        sp.dma_start(ln_g, bcast(ln1_g[bass.ds(layer, 1)].rearrange("a n -> (a n)"))).then_inc(norm_landed.sem, 16)
                        sp.dma_start(ln_b, bcast(ln1_b[bass.ds(layer, 1)].rearrange("a n -> (a n)"))).then_inc(norm_landed.sem, 16)
                        sp.dma_start(gate_b.rearrange("p a n -> p (a n)"),
                                     bcast(b_ple_gate[bass.ds(layer, 1)].rearrange("a n -> (a n)"))).then_inc(bias_landed.sem, 16)
                    if s == 8:
                        sp.wait_ge(down_free.sem, down_free.at(layer, -3))
                        for i, v in enumerate((out_norm_a, out_norm_b)):
                            sp.dma_start(o_gain[:, i, :],
                                         bcast(v[bass.ds(layer, 1)].rearrange("a n -> (a n)"))).then_inc(o_gain_landed.sem, 16)
                    if s == 20:
                        sp.wait_ge(tr_full.sem, tr_full.at(layer, TR["rot", 2, TT - 1] + 1))
                        for i, v in enumerate((p_prompt, p_sample)):
                            sp.dma_start(p_in[:, 2 * i:2 * i + 2, :],
                                         v[bass.ds(layer, 1), 0].rearrange("a (t p) n -> p (a t) n", p=P)).then_inc(p_landed.sem, 16)
                    raw_free(s)
                    load(s, source(s, layer), 2)
                sp.wait_ge(ln_done.sem, ln_done.at(layer, 4))
                sp.dma_start(ln_g, bcast(ln2_g[bass.ds(layer, 1)].rearrange("a n -> (a n)"))).then_inc(norm_landed.sem, 16)
                sp.dma_start(ln_b, bcast(ln2_b[bass.ds(layer, 1)].rearrange("a n -> (a n)"))).then_inc(norm_landed.sem, 16)
                with sp.Fori(0, FT // 2) as i:
                    for v in range(4):
                        sp.wait_ge(w_split.sem, w_split.at(layer, UP_AT + v - AHEAD - RAW + 1) + i * 4)
                        load(UP_AT + v, up_source(layer, i * 2 + v // 2, v % 2), 8)
                raw_free(DOWN_AT)
                load(DOWN_AT, down_source(layer, LOOPED), 1)
                with sp.Fori(0, LOOPED // 2) as i:
                    for v in range(2):
                        s = DOWN_AT + 1 + v
                        sp.wait_ge(w_split.sem, w_split.at(layer, s - AHEAD - RAW + 1) + i * 2)
                        load(s, down_source(layer, i * 2 + v), 1)
                for r in range(1, REST):
                    raw_free(DOWN_AT + LOOPED + r)
                    load(DOWN_AT + LOOPED + r, down_source(layer, LOOPED + r), 1)
                following = (layer + 1) % DEPTH
                for s in range(AHEAD):
                    raw_free(STREAM + s)
                    load(s, source(s, following), 2)
            for t in range(TT):
                dst = (y_prompt, y_sample)[t // 2][0, t % 2 * P:(t % 2 + 1) * P, :]
                if t == TT - 1:
                    sp.wait_ge(ln_half.sem, ln_half.at(DEPTH - 1, 1))
                    sp.dma_start(dst[:, 0:512], x[:, t, 0:512]).then_inc(y_stored.sem, 16)
                sp.wait_ge(ln_done.sem, ln_done.at(DEPTH - 1, 4 + t + 1))
                at = 512 if t == TT - 1 else 0
                sp.dma_start(dst[:, at:], x[:, t, at:]).then_inc(y_stored.sem, 16)
            sp.wait_ge(y_stored.sem, 16 * (TT + 1))
            for b in range(RAW):
                sp.wait_ge(raw_landed[b].sem, raw_landed[b].at(DEPTH, 0))

        @block.gpsimd
        def _(pool):
            pool.memset(ident[:, :], 0.0)
            pool.memset(ident_b[:, :], 0.0)
            pool.memset(mask[:, :], 0.0)
            pool.memset(half_neg[:, :], -0.5)
            pool.memset(ln_eps[:, :], LN_EPS)
            pool.drain()
            pool.affine_select(out=ident[:, :], in_=ident[:, :], compare_op=ALU.not_equal, fill=1.0,
                               base=0, pattern=[[-1, P]], channel_multiplier=1)
            pool.affine_select(out=ident_b[:, :], in_=ident_b[:, :], compare_op=ALU.not_equal, fill=1.0,
                               base=0, pattern=[[-1, P]], channel_multiplier=1)
            pool.affine_select(out=mask[:, :], in_=mask[:, :], compare_op=ALU.is_ge, fill=MASKED,
                               base=0, pattern=[[-1, P]], channel_multiplier=1)
            pool.drain().then_inc(const_made.sem, 1)

            def lo(n, value):
                pool.wait_ge(w_hi_done.sem, value)
                pool.tensor_tensor(w_lo[:, n, :], raw[:, n % RAW, :], w_hi[:, n, :].bitcast(F32),
                                   ALU.subtract).then_inc(w_split.sem, 1)

            def ln_root(t, value):
                pool.wait_ge(ln_var.sem, value)
                pool.tensor_tensor(ln_r[:, t:t + 1], mv[:, t, 1:2], half_neg[:, 0:1], ALU.pow).then_inc(ln_rstd.sem, 1)

            def first_lo(s):
                pool.wait_ge(w_hi_done.sem, s + 1)
                pool.tensor_tensor(w_lo[:, s, :], first_raw(s), w_hi[:, s, :].bitcast(F32), ALU.subtract).then_inc(w_split.sem, 1)

            ln_root(0, 1)
            ln_root(1, 2)
            first_lo(0)
            first_lo(1)
            ln_root(2, 3)
            first_lo(2)
            first_lo(3)
            ln_root(3, 4)

            with pool.Fori(0, DEPTH) as layer:
                def body_lo(s):
                    lo(s % SLOTS, w_hi_done.at(layer, s - AHEAD + 1))

                def o_root(kind, s):
                    for qt in range(2):
                        n = kind * 4 + s * 2 + qt
                        pool.wait_ge(o_ss.sem, o_ss.at(layer, n + 1))
                        pool.tensor_tensor(oss[:, qt:qt + 1], oss[:, qt:qt + 1], ln_eps[:, :], ALU.add)
                        pool.drain()
                        pool.tensor_tensor(oss[:, qt:qt + 1], oss[:, qt:qt + 1], half_neg[:, 0:1],
                                           ALU.pow).then_inc(o_rstd.sem, 1)

                for c in range(2):
                    for t in range(TT):
                        n = c * TT + t
                        w = (HEADS, KV)[c]
                        if c == 0:
                            body_lo(4 + n)
                        pool.wait_ge(qk_ss.sem, qk_ss.at(layer, n + 1))
                        pool.tensor_tensor(rqk[:, c, t, 0:w], rqk[:, c, t, 0:w], half_neg[:, 0:w],
                                           ALU.pow).then_inc(qk_rstd.sem, 1)
                        if c == 1:
                            body_lo(4 + n)
                for g in range(GROUPS + 3):
                    if g in (2, 4, 6, 8):
                        body_lo(12 + (g - 2) // 2)
                    if g in (17, 18, 21, 22):
                        body_lo(16 + (g - 17) // 4 * 2 + (g - 17) % 4)
                    if g in (30, 31):
                        body_lo(20 + g - 30)
                    if g in (11, 19, 27):
                        o_root((g - 11) // 8 // 2, (g - 11) // 8 % 2)
                o_root(1, 1)
                body_lo(22)
                body_lo(23)
                ln_root(0, ln_var.at(layer, 1))
                body_lo(24)
                body_lo(25)
                for t in range(1, TT):
                    ln_root(t, ln_var.at(layer, t + 1))
                for s in range(26, 38):
                    body_lo(s)
                with pool.Fori(0, LOOPED // 4) as i:
                    for v in range(8):
                        lo((38 + v) % SLOTS, w_hi_done.at(layer, 38 + v - AHEAD + 1) + i * 8)
                for s in range(38 + 2 * LOOPED, DOWN_AT + 6):
                    body_lo(s)
                with pool.Fori(0, LOOPED // 8) as i:
                    for v in range(8):
                        lo((DOWN_AT + 6 + v) % SLOTS, w_hi_done.at(layer, DOWN_AT + 6 + v - AHEAD + 1) + i * 8)
                body_lo(STREAM)
                body_lo(STREAM + 1)
                ln_root(0, ln_var.at(layer, 5))
                ln_root(1, ln_var.at(layer, 6))
                ln_root(2, ln_var.at(layer, 7))
                body_lo(STREAM + 2)
                body_lo(STREAM + 3)
                ln_root(3, ln_var.at(layer, 8))

        @block.scalar
        def _(act):
            def hi(n, landed, used):
                act.wait_ge(raw_landed[n % RAW].sem, landed)
                act.wait_ge(w_used.sem, used)
                act.activation(w_hi[:, n, :], raw[:, n % RAW, :], ACT.Copy).then_inc(w_hi_done.sem, 1)

            def norm_hi(t, full):
                for b in range(2):
                    act.wait_ge(tr_full.sem, full + b)
                    act.activation(xt_hi[:, 4 * b:4 * b + 4, t * P:(t + 1) * P],
                                   ps[:, TRB + b, :].rearrange("p (k n) -> p k n", k=4), ACT.Copy).then_inc(xt_hi_done.sem, 1)

            def first_hi(s):
                landed = raw_landed[s] if s < RAW else stage_landed[s - RAW]
                act.wait_ge(landed.sem, 16)
                act.activation(w_hi[:, s, :], first_raw(s), ACT.Copy).then_inc(w_hi_done.sem, 1)

            first_hi(0)
            norm_hi(0, 1)
            first_hi(1)
            first_hi(2)
            norm_hi(1, 3)
            first_hi(3)

            with act.Fori(0, DEPTH) as layer:
                def body_hi(s):
                    hi(s % SLOTS, raw_landed[s % RAW].at(layer, 16 * ((s - AHEAD) // RAW + 1)), w_used.at(layer, s - SLOTS + 1))

                def looped_hi(s, i):
                    hi(s % SLOTS, raw_landed[s % RAW].at(layer, 16 * ((s - AHEAD) // RAW + 1)) + i * (16 * 8 // RAW),
                       w_used.at(layer, s - SLOTS + 1) + i * 8)

                def win(c, t):
                    n = c * TT + t
                    bank = ps[:, n % 2, :]
                    wait_win(act, layer, c, t)
                    if c == 0:
                        act.wait_ge(ln_done.sem, ln_done.at(layer, 0))
                        if n >= 2:
                            act.wait_ge(qk_ss.sem, qk_ss.at(layer, n - 1))
                        act.activation(squares[:, n % 2, :], bank, ACT.Square).then_inc(win_act.sem, 1)
                    elif c == 1:
                        act.wait_ge(qk_ss.sem, qk_ss.at(layer, n - 1))
                        act.activation(vbuf[:, 0, t, :], bank[:, 128:256], ACT.Copy)
                        act.activation(squares[:, n % 2, 0:128], bank[:, 0:128], ACT.Square).then_inc(win_act.sem, 1)
                    else:
                        act.activation(vbuf[:, 1, t, :], bank[:, 384:512], ACT.Copy).then_inc(win_act.sem, 1)

                def qkt_evac(c, t):
                    u = TR["rot", c, t]
                    cols_t = slice(t * P, (t + 1) * P)
                    act.wait_ge(tr_full.sem, tr_full.at(layer, u + 1))
                    if c:
                        src, hi_at, _ = k_parts(c, u)
                        act.activation(k_split[:, hi_at, cols_t], src, ACT.Copy)
                    for odd in range(2):
                        src, a, b = q_parts(c, u, odd)
                        ins = act.activation(stat[HD * odd:HD * odd + HD, a, b, cols_t], src, ACT.Copy)
                    ins.then_inc(qkt_hi.sem, 1)

                def exps(g):
                    kind, s, h = group(g)
                    act.wait_ge(max_done.sem, max_done.at(layer, g + 1))
                    if g >= 2:
                        act.wait_ge(tr_full.sem, tr_full.at(layer, TR["probs_t", g - 2] + 1))
                    for qt in range(2):
                        scale = 0.125 if kind else rqk[:, 0, 2 * s + qt, h:h + 1]
                        ins = act.activation(probs[:, g % 2, qt * 256:(qt + 1) * 256],
                                             ps[:, SC + g % 2, qt * 256:(qt + 1) * 256], ACT.Exp,
                                             bias=neg_max[:, kind, s, qt, h:h + 1], scale=scale,
                                             accum_out=den[:, kind, s, qt, h:h + 1])
                    ins.then_inc(exp_done.sem, 1)

                def probs_evac(g):
                    u = TR["probs_t", g]
                    act.wait_ge(tr_full.sem, tr_full.at(layer, u + 1))
                    if g >= 2:
                        act.wait_ge(pv_done.sem, pv_done.at(layer, g - 1))
                    act.activation(probs_t[:, g % 2, :], ps[:, TRB + u % 2, :], ACT.Copy).then_inc(pt_act.sem, 1)

                def o_squares(kind, s):
                    for qt in range(2):
                        if qt:
                            act.drain()
                        act.wait_ge(o_evac.sem, o_evac.at(layer, kind * 4 + s * 2 + qt + 1))
                        act.activation(unused[:, :], heads_o[:, qt, :], ACT.Square, scale=512 ** -0.5,
                                       accum_out=oss[:, qt:qt + 1]).then_inc(o_ss.sem, 1)

                def heads_hi(kind, s, qt):
                    u = TR["heads_t", kind, s, qt]
                    t = 2 * s + qt
                    act.wait_ge(tr_full.sem, tr_full.at(layer, u + 1))
                    ins = act.activation(s_hi[:, 4 * kind:4 * kind + 4, t * P:(t + 1) * P],
                                         ps[:, TRB + u % 2, :].rearrange("p (k n) -> p k n", k=4), ACT.Copy)
                    ins.then_inc(ot_hi.sem, 1)

                def ple_evac(n, t):
                    wait_ple(act, layer, n, t)
                    act.activation(ple[:, n * TT + t, :], ps[:, SC + t % 2, :], ACT.Copy).then_inc(ple_free.sem, 1)

                def gate(n, t):
                    q = n * TT + t
                    act.wait_ge(gate_in.sem, gate_in.at(layer, q + 1))
                    act.activation(heads_o[:, q % 2, :], heads_o[:, q % 2, :], ACT.Tanh, scale=0.5).then_inc(gate_tanh.sem, 1)

                def conv_centre(bank, j, dst, n):
                    wait_up(act, layer, 0, n)
                    act.activation(dst, ps[:, bank, :], ACT.Identity, bias=conv_b[:, bass.ds(j, 1)],
                                   scale=conv_w[:, 1, bass.ds(j, 1)]).then_inc(conv_mid.sem, 1)

                def gelu(dst, n):
                    act.wait_ge(conv_done.sem, conv_done.at(layer, 1) + n)
                    act.sem_inc(gelu_begun.sem, 1)
                    act.activation(dst, dst, ACT.Gelu_apprx_tanh).then_inc(gelu_done.sem, 1)

                act.wait_ge(const_landed.sem, const_landed.at(layer, 64))
                for c in range(2):
                    for t in range(TT):
                        n = c * TT + t
                        body_hi(4 + n)
                        if n == 2:
                            qkt_evac(0, 0)
                        win(c, t)
                        if n < 2:
                            norm_hi(n + 2, tr_full.at(layer, TR["norm_in", n + 2] + 1))
                        else:
                            qkt_evac(*divmod(n - 1, TT))
                for g in range(GROUPS + 3):
                    if g == 2:
                        qkt_evac(1, 3)
                    if g in (6, 10, 14, 18):
                        qkt_evac(2, (g - 6) // 4)
                    if g in (15, 16, 23, 24, 31, 32):
                        heads_hi((g - 15) // 16, (g - 15) // 8 % 2, (g - 15) % 8)
                    if g in (3, 7, 11, 15):
                        win(2, (g - 3) // 4)
                    if g in (29, 30):
                        k = g - 29
                        act.wait_ge(tr_full.sem, tr_full.at(layer, TR["p_t", k] + 1))
                        act.activation(xt_hi[:, k, :], ps[:, TRB + TR["p_t", k] % 2, :], ACT.Copy,
                                       scale=0.5).then_inc(p_hi.sem, 1)
                    if g < GROUPS:
                        exps(g)
                    if 2 <= g < GROUPS + 2 and g % 2:
                        probs_evac(g - 2)
                    if g in (2, 4, 6, 8):
                        body_hi(12 + (g - 2) // 2)
                    if g in (17, 18, 21, 22):
                        body_hi(16 + (g - 17) // 4 * 2 + (g - 17) % 4)
                    if g in (30, 31):
                        body_hi(20 + g - 30)
                    if g in (24, 32):
                        n = (g - 24) // 8
                        act.wait_ge(sink_in.sem, sink_in.at(layer, n + 1))
                        act.activation(sink_e[:, :, :], sink_e[:, :, :], ACT.Exp).then_inc(sink_exp.sem, 1)
                    if g in (33, 34):
                        ple_evac(0, g - 33)
                    if g in (10, 18, 26, 34):
                        n = (g - 10) // 8
                        o_squares(n // 2, n % 2)
                ple_evac(0, 2)
                ple_evac(0, 3)
                body_hi(22)
                body_hi(23)
                heads_hi(1, 1, 0)
                heads_hi(1, 1, 1)
                for t in range(TT):
                    ple_evac(1, t)
                body_hi(24)
                body_hi(25)
                norm_hi(0, tr_full.at(layer, TR["norm1", 0] + 1))
                norm_hi(1, tr_full.at(layer, TR["norm1", 1] + 1))
                body_hi(26)
                body_hi(27)
                norm_hi(2, tr_full.at(layer, TR["norm1", 2] + 1))
                gate(0, 0)
                body_hi(28)
                norm_hi(3, tr_full.at(layer, TR["norm1", 3] + 1))
                gate(0, 1)
                body_hi(29)
                gate(0, 2)
                gate(0, 3)
                gate(1, 0)
                body_hi(30)
                body_hi(31)
                gate(1, 1)
                body_hi(32)
                gate(1, 2)
                body_hi(33)
                gate(1, 3)
                for s in range(34, 38):
                    body_hi(s)

                with act.Fori(0, LOOPED // 4) as i:
                    for v in range(4):
                        dst = hbuf[:, bass.ds(i * 4 + v, 1), :].rearrange("p a n -> p (a n)")
                        conv_centre(2 * (v % 2), i * 4 + v, dst, i * 4 + v)
                        looped_hi(38 + 2 * v, i)
                        gelu(dst, i * 4 + v)
                        looped_hi(39 + 2 * v, i)
                for r in range(REST):
                    j = LOOPED + r
                    dst = scratch[:, 4 + r % 2, :]
                    if r >= 2:
                        act.wait_ge(h_rest_split.sem, h_rest_split.at(layer, r - 1))
                    conv_centre(2 * (j % 2), j, dst, j)
                    if j < FT - 1:
                        body_hi(38 + 2 * j)
                    gelu(dst, j)
                    if j < FT - 1:
                        body_hi(39 + 2 * j)
                    act.wait_ge(h_done.sem, h_done.at(layer, j + 1))
                    act.activation(s_hi[:, r, :], dst, ACT.Copy).then_inc(h_rest_hi.sem, 1)
                with act.Fori(0, LOOPED // 8) as i:
                    for v in range(8):
                        act.wait_ge(w_used.sem, w_used.at(layer, DOWN_AT + v) + i * 8)
                        act.activation(s_hi[:, 6 + v % 2, :], hbuf[:, bass.ds(i * 8 + v, 1), :].rearrange("p a n -> p (a n)"),
                                       ACT.Copy).then_inc(h_hi.sem, 1)
                        looped_hi(DOWN_AT + 6 + v, i)
                body_hi(STREAM)
                body_hi(STREAM + 1)
                norm_hi(0, tr_full.at(layer, TR["norm2", 0] + 1))
                norm_hi(1, tr_full.at(layer, TR["norm2", 1] + 1))
                body_hi(STREAM + 2)
                body_hi(STREAM + 3)

        @block.vector
        def _(dve):
            def norm_stats(t):
                for b in range(2):
                    dve.bn_stats(bn[:, b, :], x[:, t, b * 512:(b + 1) * 512])
                norm_variance(t)

            def norm_variance(t):
                dve.drain()
                dve.bn_aggr(mv[:, t, :], bn[:, :, :].rearrange("p a n -> p (a n)"))
                dve.drain()
                dve.tensor_scalar(mv[:, t, 1:2], mv[:, t, 1:2], LN_EPS, None, ALU.add).then_inc(ln_var.sem, 1)

            def norm_centre(t):
                dve.scalar_tensor_tensor(out=x[:, t, :], in0=x[:, t, :], scalar=mv[:, t, 0:1], in1=ln_g,
                                         op0=ALU.subtract, op1=ALU.mult)
                dve.drain()

            def norm_scale(t, rstd):
                dve.wait_ge(ln_rstd.sem, rstd)
                dve.scalar_tensor_tensor(out=x[:, t, :], in0=x[:, t, :], scalar=ln_r[:, t:t + 1], in1=ln_b,
                                         op0=ALU.mult, op1=ALU.add).then_inc(ln_done.sem, 1)

            def norm_apply(t, rstd, landed):
                dve.wait_ge(norm_landed.sem, landed)
                norm_centre(t)
                norm_scale(t, rstd)

            def norm_lo(t, hi):
                for b in range(2):
                    dve.wait_ge(xt_hi_done.sem, hi + b)
                    dve.tensor_tensor(xt_lo[:, 4 * b:4 * b + 4, t * P:(t + 1) * P],
                                      ps[:, TRB + b, :].rearrange("p (k n) -> p k n", k=4),
                                      xt_hi[:, 4 * b:4 * b + 4, t * P:(t + 1) * P].bitcast(F32),
                                      ALU.subtract).then_inc(xt_split.sem, 1)

            for t in range(TT):
                dve.wait_ge(x_landed[t].sem, 16)
                norm_stats(t)
                if t == 0:
                    dve.wait_ge(first_gain_landed.sem, 16)
                norm_centre(t)
                if t == 0:
                    dve.wait_ge(norm_landed.sem, 16)
                norm_scale(t, t + 1)
                if t in (1, 2):
                    norm_lo(t - 1, 2 * t - 1)
            dve.wait_ge(fixed_landed.sem, 16)

            with dve.Fori(0, DEPTH) as layer:
                def turn(v, heads, bank_cols, cs, sn, t):
                    src = v.rearrange("p (h d) -> p h d", h=heads)
                    swapped = v.rearrange("p (h i b) -> p h i b", h=heads, b=2)[:, :, :, ::-1]
                    shape = [P, heads, HD]
                    a = t1[:, bank_cols].rearrange("p (h d) -> p h d", h=heads)
                    b = t2[:, bank_cols].rearrange("p (h i b) -> p h i b", h=heads, b=2)
                    dve.tensor_tensor(a, src, cs[:, t % 2, :].unsqueeze(1).to_broadcast(shape), ALU.mult)
                    return dve.tensor_tensor(b, swapped,
                                             sn[:, t % 2, :].rearrange("p (i b) -> p i b", b=2).unsqueeze(1)
                                             .to_broadcast([P, heads, HD // 2, 2]), ALU.mult)

                def rotate(c, t):
                    n = c * TT + t
                    bank = ps[:, n % 2, :]
                    out = rot[:, n % 2, :]
                    dve.wait_ge(win_act.sem, win_act.at(layer, n + 1))
                    if n >= 2:
                        c2, tt2 = divmod(n - 2, TT)
                        dve.wait_ge(tr_full.sem, tr_full.at(layer, TR["rot", c2, tt2] + 1))
                    if c < 2:
                        w = (HEADS, KV)[c]
                        dve.tensor_reduce(rqk[:, c, t, 0:w], squares[:, n % 2, 0:w * HD].rearrange("p (h d) -> p h d", h=w),
                                          AX_X, ALU.add)
                        dve.drain()
                        dve.tensor_scalar(rqk[:, c, t, 0:w], rqk[:, c, t, 0:w], HD * QK_EPS, None,
                                          ALU.add).then_inc(qk_ss.sem, 1)
                    if c == 0:
                        turn(bank, HEADS, slice(0, 512), rope_a[:, 0], rope_a[:, 1], t).then_inc(win_free.sem, 1)
                        dve.drain()
                        dve.tensor_tensor(out, t1, t2, ALU.add).then_inc(rot_done.sem, 1)
                    elif c == 1:
                        turn(bank[:, 0:128], KV, slice(0, 128), rope_a[:, 2], rope_a[:, 3], t)
                        turn(bank[:, 256:512], 4, slice(256, 512), rope_sb[:, 2], rope_sb[:, 3], t).then_inc(win_free.sem, 1)
                        dve.drain()
                        dve.tensor_tensor(out[:, 256:512], t1[:, 256:512], t2[:, 256:512], ALU.add)
                        dve.tensor_tensor(t1[:, 0:128], t1[:, 0:128], t2[:, 0:128], ALU.add)
                        dve.drain()
                        dve.wait_ge(qk_rstd.sem, qk_rstd.at(layer, n + 1))
                        shape = [P, KV, 2, HD]
                        dve.tensor_tensor(out[:, 0:256].rearrange("p (v e d) -> p v e d", v=KV, e=2),
                                          t1[:, 0:128].rearrange("p (v d) -> p v d", v=KV).unsqueeze(2).to_broadcast(shape),
                                          rqk[:, 1, t, 0:KV].unsqueeze(2).unsqueeze(3).to_broadcast(shape),
                                          ALU.mult).then_inc(rot_done.sem, 1)
                    else:
                        turn(bank[:, 0:384], 6, slice(0, 384), rope_sb[:, 2], rope_sb[:, 3], t).then_inc(win_free.sem, 1)
                        dve.drain()
                        dve.tensor_tensor(out[:, 0:256], t1[:, 0:256], t2[:, 0:256], ALU.add)
                        shape = [P, KV, 2, HD]
                        dve.tensor_tensor(out[:, 256:512].rearrange("p (v e d) -> p v e d", v=KV, e=2),
                                          t1[:, 256:384].rearrange("p (v d) -> p v d", v=KV).unsqueeze(2).to_broadcast(shape),
                                          t2[:, 256:384].rearrange("p (v d) -> p v d", v=KV).unsqueeze(2).to_broadcast(shape),
                                          ALU.add).then_inc(rot_done.sem, 1)

                def qkt_lo(c, t):
                    u = TR["rot", c, t]
                    cols_t = slice(t * P, (t + 1) * P)
                    dve.wait_ge(qkt_hi.sem, qkt_hi.at(layer, c * TT + t + 1))
                    if c:
                        src, hi_at, lo_at = k_parts(c, u)
                        dve.tensor_tensor(k_split[:, lo_at, cols_t], src, k_split[:, hi_at, cols_t].bitcast(F32), ALU.subtract)
                    for odd in range(2):
                        src, a, b = q_parts(c, u, odd)
                        ins = dve.tensor_tensor(stat[HD * (1 - odd):HD * (1 - odd) + HD, a, b, cols_t], src,
                                                stat[HD * odd:HD * odd + HD, a, b, cols_t].bitcast(F32), ALU.subtract)
                    ins.then_inc(qkt_done.sem, 1)

                def maxima(g):
                    kind, s, h = group(g)
                    mx = row_max[:, g % 2, :]
                    dve.wait_ge(sc_full.sem, sc_full.at(layer, g + 1))
                    dve.tensor_reduce(mx, ps[:, SC + g % 2, :].rearrange("p (q n) -> p q n", q=2), AX_X, ALU.max)
                    dve.drain()
                    if g == 0:
                        dve.wait_ge(qk_rstd.sem, qk_rstd.at(layer, 2 * TT))
                    if kind == 0:
                        dve.scalar_tensor_tensor(out=neg_max[:, 0, s, :, h], in0=mx, scalar=-1.0,
                                                 in1=rqk[:, 0, 2 * s:2 * s + 2, h], op0=ALU.mult,
                                                 op1=ALU.mult).then_inc(max_done.sem, 1)
                    else:
                        dve.tensor_scalar(neg_max[:, 1, s, :, h], mx, -0.125, neg_sinks[:, h:h + 1], ALU.mult,
                                          ALU.min).then_inc(max_done.sem, 1)

                def probs_evac(g):
                    u = TR["probs_t", g]
                    dve.wait_ge(tr_full.sem, tr_full.at(layer, u + 1))
                    if g >= 2:
                        dve.wait_ge(pv_done.sem, pv_done.at(layer, g - 1))
                    dve.tensor_copy(probs_t[:, g % 2, :], ps[:, TRB + u % 2, :]).then_inc(pt_dve.sem, 1)

                def heads_den(kind, s):
                    n = kind * 2 + s
                    d = den[:, kind, s, :, :]
                    dve.wait_ge(exp_done.sem, exp_done.at(layer, 8 * n + 8))
                    if kind:
                        dve.tensor_tensor(sink_e[:, :, :], neg_max[:, 1, s, :, :],
                                          sinks[:, :].unsqueeze(1).to_broadcast([P, 2, HEADS]), ALU.add).then_inc(sink_in.sem, 1)
                        dve.wait_ge(sink_exp.sem, sink_exp.at(layer, s + 1))
                        dve.tensor_tensor(d, d, sink_e[:, :, :], ALU.add)
                        dve.drain()
                    dve.reciprocal(d, d)
                    dve.drain()

                def heads_evac(kind, s):
                    n = kind * 2 + s
                    if n:
                        k2, s2 = divmod(n - 1, 2)
                        dve.wait_ge(tr_full.sem, tr_full.at(layer, TR["heads_t", k2, s2, 1] + 1))
                    dve.wait_ge(pv_done.sem, pv_done.at(layer, 8 * n + 8))
                    for qt in range(2):
                        dve.tensor_tensor(heads_o[:, qt, :].rearrange("p (h d) -> p h d", h=HEADS),
                                          ps[:, OB + qt, :].rearrange("p (h d) -> p h d", h=HEADS),
                                          den[:, kind, s, qt, :].unsqueeze(2).to_broadcast([P, HEADS, HD]),
                                          ALU.mult).then_inc(o_evac.sem, 1)

                def heads_norm(kind, s):
                    if kind == 0 and s == 0:
                        dve.wait_ge(o_gain_landed.sem, o_gain_landed.at(layer, 32))
                    for qt in range(2):
                        dve.wait_ge(o_rstd.sem, o_rstd.at(layer, kind * 4 + s * 2 + qt + 1))
                        dve.scalar_tensor_tensor(out=heads_o[:, qt, :], in0=heads_o[:, qt, :], scalar=oss[:, qt:qt + 1],
                                                 in1=o_gain[:, kind, :], op0=ALU.mult, op1=ALU.mult).then_inc(o_norm.sem, 1)

                def heads_lo(kind, s, qt):
                    u = TR["heads_t", kind, s, qt]
                    t = 2 * s + qt
                    dve.wait_ge(ot_hi.sem, ot_hi.at(layer, kind * 4 + t + 1))
                    ins = dve.tensor_tensor(s_lo[:, 4 * kind:4 * kind + 4, t * P:(t + 1) * P],
                                            ps[:, TRB + u % 2, :].rearrange("p (k n) -> p k n", k=4),
                                            s_hi[:, 4 * kind:4 * kind + 4, t * P:(t + 1) * P].bitcast(F32), ALU.subtract)
                    ins.then_inc(ot_split.sem, 1)

                def outa(t, n):
                    wait_outa(dve, layer, t, n)
                    xs = x[:, t, n * 512:(n + 1) * 512]
                    dve.scalar_tensor_tensor(out=xs, in0=xs, scalar=ALPHA, in1=ps[:, n, :], op0=ALU.mult,
                                             op1=ALU.add).then_inc(outa_free.sem, 1)

                def add_banks(t, bank, freed):
                    dve.tensor_tensor(x[:, t, :], x[:, t, :], ps[:, bank:bank + 2, :].rearrange("p a n -> p (a n)"),
                                      ALU.add).then_inc(freed.sem, 1)
                    dve.drain()

                def outb(t, between=lambda: None):
                    wait_outb(dve, layer, t)
                    add_banks(t, OUTB_BANK[t], outb_free)
                    norm_stats(t)
                    between()
                    norm_apply(t, ln_rstd.at(layer, t + 1), norm_landed.at(layer, 32))

                def gate_sum(n, t):
                    q = n * TT + t
                    wait_gate(dve, layer, n, t)
                    if q == 0:
                        dve.wait_ge(bias_landed.sem, bias_landed.at(layer, 16))
                    dve.tensor_tensor(heads_o[:, q % 2, :], ps[:, OB + q % 2, :], gate_b[:, n, :], ALU.add).then_inc(gate_in.sem, 1)

                def gate_apply(n, t):
                    q = n * TT + t
                    buf = heads_o[:, q % 2, :]
                    dve.wait_ge(gate_tanh.sem, gate_tanh.at(layer, q + 1))
                    if q == 0:
                        dve.wait_ge(ple_free.sem, ple_free.at(layer, 8))
                    dve.scalar_tensor_tensor(out=buf, in0=buf, scalar=1.0, in1=ple[:, q, :], op0=ALU.add, op1=ALU.mult)
                    dve.drain()
                    xs = x[:, t, n * 512:(n + 1) * 512]
                    dve.scalar_tensor_tensor(out=xs, in0=xs, scalar=ALPHA, in1=buf, op0=ALU.mult, op1=ALU.add)

                def conv_sides(bank, j, dst, n):
                    dve.wait_ge(conv_mid.sem, conv_mid.at(layer, 1) + n)
                    d = dst.rearrange("p (s n) -> p s n", s=2)
                    g = ps[:, bank, :].rearrange("p (s n) -> p s n", s=2)
                    dve.scalar_tensor_tensor(out=d[:, :, 1:], in0=g[:, :, 0:SEQ - 1], scalar=conv_w[:, 0, bass.ds(j, 1)],
                                             in1=d[:, :, 1:], op0=ALU.mult, op1=ALU.add)
                    dve.drain()
                    dve.scalar_tensor_tensor(out=d[:, :, 0:SEQ - 1], in0=g[:, :, 1:], scalar=conv_w[:, 2, bass.ds(j, 1)],
                                             in1=d[:, :, 0:SEQ - 1], op0=ALU.mult, op1=ALU.add).then_inc(conv_done.sem, 1)

                def glu(bank, dst, n):
                    wait_up(dve, layer, 1, n)
                    dve.wait_ge(gelu_done.sem, gelu_done.at(layer, 1) + n)
                    dve.tensor_tensor(dst, dst, ps[:, bank + 1, :], ALU.mult).then_inc(h_done.sem, 1)

                dve.wait_ge(const_landed.sem, const_landed.at(layer, 64))
                for i in range(2):
                    g = gains[:, i, :].unsqueeze(1).to_broadcast([P, 2, HD])
                    gs = (gains[:, i, :].rearrange("p (i b) -> p i b", b=2)[:, :, ::-1].unsqueeze(1)
                          .to_broadcast([P, 2, HD // 2, 2]))
                    dve.tensor_tensor(rope_a[:, 2 * i, :, :], rope_sb[:, 0, :, :], g, ALU.mult)
                    dve.tensor_tensor(rope_a[:, 2 * i + 1, :, :].rearrange("p t (i b) -> p t i b", b=2),
                                      rope_sb[:, 1, :, :].rearrange("p t (i b) -> p t i b", b=2), gs, ALU.mult)
                dve.tensor_scalar(neg_sinks[:, :], sinks[:, :], -1.0, None, ALU.mult)
                dve.drain()
                dve.tensor_scalar(rope_a[:, 2:4, :, :], rope_a[:, 2:4, :, :], 8.0, None, ALU.mult)
                dve.drain()

                norm_lo(2, xt_hi_done.at(layer, 1))
                for c in range(2):
                    for t in range(TT):
                        n = c * TT + t
                        if n == 2:
                            qkt_lo(0, 0)
                        rotate(c, t)
                        if n == 0:
                            norm_lo(3, xt_hi_done.at(layer, 3))
                        if n >= 2:
                            qkt_lo(*divmod(n - 1, TT))
                for g in range(GROUPS + 3):
                    if g < GROUPS:
                        maxima(g)
                    if g == 2:
                        qkt_lo(1, 3)
                    if g in (6, 10, 14, 18):
                        qkt_lo(2, (g - 6) // 4)
                    if g in (15, 16, 23, 24, 31, 32):
                        heads_lo((g - 15) // 16, (g - 15) // 8 % 2, (g - 15) % 8)
                    if g in (29, 30):
                        k = g - 29
                        dve.wait_ge(p_hi.sem, p_hi.at(layer, k + 1))
                        dve.scalar_tensor_tensor(out=xt_lo[:, k, :], in0=ps[:, TRB + TR["p_t", k] % 2, :], scalar=0.5,
                                                 in1=xt_hi[:, k, :].bitcast(F32), op0=ALU.mult,
                                                 op1=ALU.subtract).then_inc(p_split.sem, 1)
                    if 2 <= g < GROUPS + 2 and g % 2 == 0:
                        probs_evac(g - 2)
                    if g in (3, 7, 11, 15):
                        rotate(2, (g - 3) // 4)
                    if g in (8, 16, 24, 32):
                        n = (g - 8) // 8
                        heads_den(n // 2, n % 2)
                    if g in (10, 18, 26, 34):
                        n = (g - 10) // 8
                        heads_evac(n // 2, n % 2)
                    if g in (13, 21, 29):
                        n = (g - 13) // 8
                        heads_norm(n // 2, n % 2)
                    if 16 <= g < 32 and g % 2:
                        outa(*divmod((g - 16) // 2, 2))
                def last_heads_lo():
                    heads_lo(1, 1, 0)
                    heads_lo(1, 1, 1)

                heads_norm(1, 1)
                outb(0, last_heads_lo)
                outb(1)
                norm_lo(0, xt_hi_done.at(layer, 5))
                outb(2)
                norm_lo(1, xt_hi_done.at(layer, 7))
                outb(3)
                norm_lo(2, xt_hi_done.at(layer, 9))
                for q in range(2 * TT):
                    gate_sum(*divmod(q, TT))
                    if q == 0:
                        norm_lo(3, xt_hi_done.at(layer, 11))
                    gate_apply(*divmod(q, TT))

                with dve.Fori(0, LOOPED // 4) as i:
                    for v in range(4):
                        dst = hbuf[:, bass.ds(i * 4 + v, 1), :].rearrange("p a n -> p (a n)")
                        conv_sides(2 * (v % 2), i * 4 + v, dst, i * 4 + v)
                        glu(2 * (v % 2), dst, i * 4 + v)
                for r in range(REST):
                    j = LOOPED + r
                    dst = scratch[:, 4 + r % 2, :]
                    conv_sides(2 * (j % 2), j, dst, j)
                    glu(2 * (j % 2), dst, j)
                    dve.wait_ge(h_rest_hi.sem, h_rest_hi.at(layer, r + 1))
                    dve.tensor_tensor(s_lo[:, r, :], dst, s_hi[:, r, :].bitcast(F32), ALU.subtract).then_inc(h_rest_split.sem, 1)
                with dve.Fori(0, LOOPED // 8) as i:
                    for v in range(8):
                        dve.wait_ge(h_hi.sem, h_hi.at(layer, v + 1) + i * 8)
                        dve.tensor_tensor(s_lo[:, 6 + v % 2, :], hbuf[:, bass.ds(i * 8 + v, 1), :].rearrange("p a n -> p (a n)"),
                                          s_hi[:, 6 + v % 2, :].bitcast(F32), ALU.subtract).then_inc(h_split.sem, 1)
                for t in range(TT - 1):
                    wait_down(dve, layer, t)
                    add_banks(t, DOWN_BANK[t], down_free)
                    norm_stats(t)
                    norm_apply(t, ln_rstd.at(layer, 4 + t + 1), norm_landed.at(layer, 64))
                    if t in (1, 2):
                        norm_lo(t - 1, xt_hi_done.at(layer, 13 + 2 * (t - 1)))
                t = TT - 1
                for n in range(2):
                    if n == 0:
                        dve.wait_ge(down_full.sem, down_full.at(layer, 4))
                    else:
                        dve.wait_ge(w_used.sem, w_used.at(layer, STREAM))
                    half = x[:, t, n * 512:(n + 1) * 512]
                    ins = dve.tensor_tensor(half, half, ps[:, DOWN_BANK[t] + n, :], ALU.add)
                    if n:
                        ins.then_inc(down_free.sem, 1)
                    dve.drain()
                    dve.bn_stats(bn[:, n, :], half)
                norm_variance(t)
                norm_centre(t)
                dve.wait_ge(ln_rstd.sem, ln_rstd.at(layer, 8))
                for n in range(2):
                    half = slice(n * 512, (n + 1) * 512)
                    dve.scalar_tensor_tensor(out=x[:, t, half], in0=x[:, t, half], scalar=ln_r[:, t:t + 1], in1=ln_b[:, half],
                                             op0=ALU.mult, op1=ALU.add).then_inc((ln_done if n else ln_half).sem, 1)

        @block.tensor
        def _(pe):
            def product(out, a, b, first, last):
                pe.matmul(out, a[0], b[0], start=first, stop=False)
                pe.matmul(out, a[0], b[1], start=False, stop=False)
                return pe.matmul(out, a[1], b[0], start=False, stop=last)

            def norm_t(t, ready):
                pe.wait_ge(ln_done.sem, ready)
                for b in range(2):
                    yield b
                    for k in range(4):
                        ins = pe.transpose(ps[:, TRB + b, k * P:(k + 1) * P], x[:, t, (4 * b + k) * P:(4 * b + k + 1) * P],
                                           ident[:, :])
                    ins.then_inc(tr_full.sem, 1)

            def xt(k, t):
                return xt_hi[:, k, t * P:(t + 1) * P], xt_lo[:, k, t * P:(t + 1) * P]

            pe.sem_inc(w_used.sem, SLOTS)
            pe.sem_inc(h_done.sem, 2)
            pe.sem_inc(down_free.sem, 4)
            def keep_warm(rounds):
                with pe.Fori(0, rounds) as _:
                    for _ in range(8):
                        pe.matmul(ps[:, 0, 0:P], ident_b[:, :], mask[:, :], start=True, stop=True)

            pe.wait_ge(const_made.sem, 1)
            keep_warm(WARM[0])
            for t in range(2):
                for b in norm_t(t, t + 1):
                    if t:
                        pe.wait_ge(xt_split.sem, b + 1)
                if t == 0:
                    keep_warm(WARM[1])

            with pe.Fori(0, DEPTH) as layer:
                def split(s):
                    pe.wait_ge(w_split.sem, w_split.at(layer, s - AHEAD + 1))

                def body_norm_t(t, step, ready):
                    for b in norm_t(t, ready):
                        wait_bank(TR[step] + b)

                def wait_bank(u):
                    before = [s for s, n in TR.items() if n == u - 2 or (s[0].startswith("norm") and n == u - 3)]
                    if not before:
                        pe.wait_ge(xt_split.sem, xt_split.at(layer, u % 2 - 1))
                        return
                    s = before[0]
                    if s[0] == "norm_in":
                        pe.wait_ge(xt_split.sem, xt_split.at(layer, 2 * (s[1] - 2) + u - 2 - TR[s] + 1))
                    elif s[0] == "norm1":
                        pe.wait_ge(xt_split.sem, xt_split.at(layer, 4 + 2 * s[1] + u - 2 - TR[s] + 1))
                    elif s[0] == "norm2":
                        pe.wait_ge(xt_split.sem, xt_split.at(layer, 12 + 2 * s[1] + u - 2 - TR[s] + 1))
                    elif s[0] == "rot":
                        pe.wait_ge(qkt_done.sem, qkt_done.at(layer, s[1] * TT + s[2] + 1))
                    elif s[0] == "p_t":
                        pe.wait_ge(p_split.sem, p_split.at(layer, s[1] + 1))
                    elif s[0] == "probs_t":
                        done = pt_act if s[1] % 2 else pt_dve
                        pe.wait_ge(done.sem, done.at(layer, s[1] // 2 + 1))
                    else:
                        pe.wait_ge(ot_split.sem, ot_split.at(layer, s[1] * 4 + s[2] * 2 + s[3] + 1))

                def win_quarter(c, t, q):
                    n = c * TT + t
                    if t == 0:
                        split(IN_AT + 4 * c + q)
                    if q == 0:
                        if c < 2:
                            pe.wait_ge(xt_split.sem, 16 * layer + 2 * t + 2)
                        if n >= 2:
                            pe.wait_ge(win_free.sem, win_free.at(layer, n - 1))
                        else:
                            pe.wait_ge(down_free.sem, down_free.at(layer, -1))
                    b = slot(IN_AT + 4 * c + q)
                    for k in range(2):
                        ins = product(ps[:, n % 2, :], xt(2 * q + k, t), (b[0][:, k, :], b[1][:, k, :]),
                                      q == 0 and k == 0, q == 3 and k == 1)
                    return ins

                def out_quarter(half, t, n, q, bank):
                    s = (OUTB_AT if half else OUT_AT) + 2 * n + q
                    if t == 0:
                        split(s)
                    b = slot(s)
                    for k in range(2):
                        kk = 4 * half + 2 * q + k
                        ins = product(ps[:, bank, :], (s_hi[:, kk, t * P:(t + 1) * P], s_lo[:, kk, t * P:(t + 1) * P]),
                                      (b[0][:, k, :], b[1][:, k, :]), q == 0 and k == 0, q == 1 and k == 1)
                    return ins

                def signal(ins, full, closes, t):
                    if t == TT - 1:
                        ins.then_inc(w_used.sem, 1)
                    elif closes:
                        ins.then_inc(full.sem, 1)

                for step in STEPS:
                    kind = step[0]
                    if kind == "win":
                        _, c, t, half = step
                        for q in (2 * half, 2 * half + 1):
                            ins = win_quarter(c, t, q)
                            signal(ins, win_full, q == 3, t)
                    elif kind == "win_part":
                        t, q = divmod(step[1], 4)
                        ins = win_quarter(2, t, q)
                        signal(ins, win_full, q == 3, t)
                    elif kind == "norm_in":
                        body_norm_t(step[1], step, ln_done.at(layer, step[1] - 3))
                    elif kind == "rot":
                        _, c, t = step
                        u = TR[step]
                        pe.wait_ge(rot_done.sem, rot_done.at(layer, c * TT + t + 1))
                        wait_bank(u)
                        for k in range(4):
                            ins = pe.transpose(ps[:, TRB + u % 2, k * P:(k + 1) * P], rot[:, t % 2, k * P:(k + 1) * P], ident[:, :])
                        ins.then_inc(tr_full.sem, 1)
                    elif kind == "scores":
                        g = step[1]
                        k, seq, h = group(g)
                        if g < 2:
                            pe.wait_ge(down_free.sem, down_free.at(layer, 0))
                        else:
                            pe.wait_ge(exp_done.sem, exp_done.at(layer, g - 1))
                        if g % 8 == 0:
                            pe.wait_ge(qkt_done.sem, qkt_done.at(layer, TT * (1 + k) + 2 * seq + 2))
                        rows = slice(HD * (h % 2), HD * (h % 2) + HD)
                        a, b = q_stack(k, h)
                        keys = slice(seq * SEQ, (seq + 1) * SEQ)
                        for qt in range(2):
                            t = 2 * seq + qt
                            out = ps[:, SC + g % 2, qt * 256:(qt + 1) * 256]
                            pe.matmul(out, stat[:, a, b, t * P:(t + 1) * P], k_split[:, k_block(k, h // 4, 0), keys],
                                      start=True, stop=False, skip_group_check=True)
                            ins = pe.matmul(out, stat[rows, a, b, t * P:(t + 1) * P], k_split[rows, k_block(k, h // 4, 1), keys],
                                            start=False, stop=(k == 0), skip_group_check=True)
                            if k:
                                m1, m2 = (mask, ident_b) if qt else (ident_b, mask)
                                ins = pe.matmul(out[:, (1 - qt) * P:(2 - qt) * P], m1[:, :], m2[:, :],
                                                start=False, stop=True, skip_group_check=True)
                        ins.then_inc(sc_full.sem, 1)
                    elif kind == "probs_t":
                        g = step[1]
                        u = TR[step]
                        pe.wait_ge(exp_done.sem, exp_done.at(layer, g + 1))
                        wait_bank(u)
                        for kb in range(2):
                            for qt in range(2):
                                ins = pe.transpose(ps[:, TRB + u % 2, kb * 256 + qt * P:kb * 256 + (qt + 1) * P],
                                                   probs[:, g % 2, qt * 256 + kb * P:qt * 256 + (kb + 1) * P], ident[:, :])
                        ins.then_inc(tr_full.sem, 1)
                    elif kind == "pv":
                        g = step[1]
                        k, s, h = group(g)
                        done = pt_act if g % 2 else pt_dve
                        pe.wait_ge(done.sem, done.at(layer, g // 2 + 1))
                        if g == 0:
                            pe.wait_ge(down_free.sem, down_free.at(layer, -2))
                        elif h == 0:
                            pe.wait_ge(o_evac.sem, o_evac.at(layer, g // 4))
                        for qt in range(2):
                            for kb in range(2):
                                ins = pe.matmul(ps[:, OB + qt, h * HD:(h + 1) * HD],
                                                probs_t[:, g % 2, kb * 256 + qt * P:kb * 256 + (qt + 1) * P],
                                                vbuf[:, k, 2 * s + kb, h // 4 * HD:(h // 4 + 1) * HD],
                                                start=(kb == 0), stop=(kb == 1))
                        ins.then_inc(pv_done.sem, 1)
                    elif kind == "heads_t":
                        _, k, s, qt = step
                        u = TR[step]
                        pe.wait_ge(o_norm.sem, o_norm.at(layer, k * 4 + s * 2 + qt + 1))
                        wait_bank(u)
                        for b in range(4):
                            ins = pe.transpose(ps[:, TRB + u % 2, b * P:(b + 1) * P], heads_o[:, qt, b * P:(b + 1) * P], ident[:, :])
                        ins.then_inc(tr_full.sem, 1)
                    elif kind == "outa_part":
                        t, r = divmod(step[1], 4)
                        n, q = divmod(r, 2)
                        if r == 0:
                            pe.wait_ge(ot_split.sem, ot_split.at(layer, t + 1))
                        if q == 0:
                            if t == 0:
                                pe.wait_ge(win_free.sem, win_free.at(layer, 11 + n))
                            else:
                                pe.wait_ge(outa_free.sem, outa_free.at(layer, 2 * t + n - 1))
                        ins = out_quarter(0, t, n, q, n)
                        signal(ins, outa_full, q == 1, t)
                    elif kind == "outb":
                        t = step[1]
                        pe.wait_ge(ot_split.sem, ot_split.at(layer, 4 + t + 1))
                        if t == 0:
                            pe.wait_ge(outa_free.sem, outa_free.at(layer, 8))
                        elif t == 1:
                            pe.wait_ge(o_evac.sem, o_evac.at(layer, 8))
                        elif t == 2:
                            pe.wait_ge(ple_free.sem, ple_free.at(layer, 8))
                        else:
                            pe.wait_ge(outb_free.sem, outb_free.at(layer, 1))
                        for n in range(2):
                            for q in range(2):
                                ins = out_quarter(1, t, n, q, OUTB_BANK[t] + n)
                                signal(ins, outb_full, n and q, t)
                    elif kind == "norm1":
                        body_norm_t(step[1], step, ln_done.at(layer, step[1] + 1))
                    elif kind == "p_t":
                        k = step[1]
                        u = TR[step]
                        if k == 0:
                            pe.wait_ge(p_landed.sem, p_landed.at(layer, 32))
                        wait_bank(u)
                        for t in range(TT):
                            ins = pe.transpose(ps[:, TRB + u % 2, t * P:(t + 1) * P], p_in[:, t, k * P:(k + 1) * P], ident[:, :])
                        ins.then_inc(tr_full.sem, 1)
                    elif kind == "ple":
                        _, n, t = step
                        i = n * TT + t
                        if t == 0:
                            split(PLE_AT + n)
                        if i == 0:
                            pe.wait_ge(p_split.sem, p_split.at(layer, KP))
                        if i < 2:
                            pe.wait_ge(exp_done.sem, exp_done.at(layer, GROUPS))
                        else:
                            pe.wait_ge(ple_free.sem, ple_free.at(layer, i - 1))
                        b = slot(PLE_AT + n)
                        for k in range(KP):
                            ins = product(ps[:, SC + t % 2, :], xt(k, t), (b[0][:, k, :], b[1][:, k, :]), k == 0, k == KP - 1)
                        signal(ins, ple_full, True, t)
                    elif kind == "gate":
                        _, n, t = step
                        i = n * TT + t
                        if n == 0:
                            pe.wait_ge(xt_split.sem, xt_split.at(layer, 4 + 2 * t + 2))
                        if i < 2:
                            pe.wait_ge(outb_free.sem, outb_free.at(layer, 2))
                        else:
                            pe.wait_ge(gate_in.sem, gate_in.at(layer, i - 1))
                        for q in range(4):
                            if t == 0:
                                split(GATE_AT + 4 * n + q)
                            b = slot(GATE_AT + 4 * n + q)
                            for k in range(2):
                                ins = product(ps[:, OB + i % 2, :], xt(2 * q + k, t), (b[0][:, k, :], b[1][:, k, :]),
                                              q == 0 and k == 0, q == 3 and k == 1)
                            signal(ins, gate_full, q == 3, t)

                def up_tile(bank, s, n):
                    pe.wait_ge(h_done.sem, h_done.at(layer, -1) + n)
                    for v in range(2):
                        pe.wait_ge(w_split.sem, w_split.at(layer, s[0] + v - AHEAD + 1) + s[1])
                        a = slot(s[0] + v, KD)
                        for k in range(KD):
                            ins = product(ps[:, bank + v, :], (a[0][:, k, :], a[1][:, k, :]), (xt_hi[:, k, :], xt_lo[:, k, :]),
                                          k == 0, k == KD - 1)
                        ins.then_inc(w_used.sem, 1)

                pe.wait_ge(xt_split.sem, xt_split.at(layer, 12))
                pe.sem_inc(ffn_begun.sem, 1)
                with pe.Fori(0, LOOPED // 4) as i:
                    for v in range(4):
                        up_tile(2 * (v % 2), (UP_AT + 2 * v, i * 8), i * 4 + v)
                for j in range(LOOPED, FT):
                    up_tile(2 * (j % 2), (UP_AT + 2 * j, 0), j)

                def down(j, s, t, first, last, halves=(0, 1)):
                    b = slot(s, 1)
                    for n in halves:
                        ins = product(ps[:, DOWN_BANK[t] + n, :], (s_hi[:, j, t * P:(t + 1) * P], s_lo[:, j, t * P:(t + 1) * P]),
                                      (b[0][:, 0, n * 512:(n + 1) * 512], b[1][:, 0, n * 512:(n + 1) * 512]), first, last)
                    return ins

                split(DOWN_AT)
                pe.wait_ge(h_rest_split.sem, h_rest_split.at(layer, 1))
                for t in range(TT):
                    if t >= 2:
                        pe.wait_ge(h_done.sem, h_done.at(layer, FT - 3 + t))
                    ins = down(0, DOWN_AT, t, True, False)
                ins.then_inc(w_used.sem, 1)
                with pe.Fori(0, LOOPED // 8) as i:
                    for v in range(8):
                        s = DOWN_AT + 1 + v
                        pe.wait_ge(h_split.sem, h_split.at(layer, v + 1) + i * 8)
                        pe.wait_ge(w_split.sem, w_split.at(layer, s - AHEAD + 1) + i * 8)
                        for t in range(TT):
                            ins = down(6 + v % 2, s, t, False, False)
                        ins.then_inc(w_used.sem, 1)
                pe.wait_ge(h_rest_split.sem, h_rest_split.at(layer, REST))
                for t in range(TT - 1):
                    for r in range(1, REST):
                        if t == 0:
                            split(DOWN_AT + LOOPED + r)
                        ins = down(r, DOWN_AT + LOOPED + r, t, False, r == REST - 1)
                        signal(ins, down_full, r == REST - 1, t)
                    if t in (1, 2):
                        if t == 1:
                            pe.wait_ge(down_free.sem, down_free.at(layer, 1))
                        body_norm_t(t - 1, ("norm2", t - 1), ln_done.at(layer, 4 + t))
                for n in range(2):
                    for r in range(1, REST):
                        ins = down(r, DOWN_AT + LOOPED + r, TT - 1, False, r == REST - 1, (n,))
                        if n:
                            ins.then_inc(w_used.sem, 1)
                        elif r == REST - 1:
                            ins.then_inc(down_full.sem, 1)


def _rope():
    pos = np.arange(SEQ, dtype=np.float32)

    def inverse(width):
        return np.float32(THETA) ** (-np.arange(0, width, 2, dtype=np.float32) / np.float32(width))

    inv2 = inverse(HD // 2)
    row, col = np.floor(pos / GRID_W).astype(np.float32), (pos % GRID_W).astype(np.float32)
    axial = np.concatenate([row[:, None] * inv2[None], col[:, None] * inv2[None]], -1)
    plain = pos[:, None] * inverse(HD)[None]
    tables = []
    for angle in (axial, plain):
        c, s = np.cos(angle), np.sin(angle)
        tables += [np.repeat(c, 2, -1), np.stack([-s, s], -1).reshape(SEQ, HD)]
    t = np.stack(tables).astype(np.float32).reshape(4, SEQ // P, P, HD)
    return np.ascontiguousarray(t.transpose(2, 0, 1, 3))


def _columns(a):
    return a.reshape(DEPTH, -1, P).transpose(0, 2, 1)


def kernel(**inputs):
    import concourse.bacc as bacc
    from concourse.bass_utils import run_bass_kernel_spmd

    nc = bacc.Bacc("TRN2", target_bir_lowering=False, num_devices=1)
    arrays, args = {}, []

    def add(name, a):
        a = np.ascontiguousarray(a)
        arrays[f"in_{name}_dram"] = a
        args.append(nc.dram_tensor(f"in_{name}_dram", a.shape, mybir.dt.from_np(a.dtype), kind="ExternalInput").ap())

    given = {k: np.asarray(v) for k, v in inputs.items()}
    for name in ("x_prompt", "x_sample", "p_prompt", "p_sample", "ln0_g", "ln0_b", "w_in", "q_norm", "k_norm", "sink",
                 "out_norm_a", "out_norm_b"):
        add(name, given[name])
    conv = given["conv_w"].reshape(DEPTH, 3, FT, P).transpose(0, 3, 1, 2).reshape(DEPTH, P, 3 * FT)
    add("columns", np.concatenate([conv, _columns(given["conv_b"])], -1))
    for name in ("w_out", "ln1_g", "ln1_b", "w_up", "w_down", "ln2_g", "ln2_b", "w_ple", "w_ple_gate", "b_ple_gate"):
        add(name, given[name])
    add("rope", _rope())
    for name in ("y_prompt", "y_sample"):
        args.append(nc.dram_tensor(f"out_{name}_dram", (1, SEQ, D), F32, kind="ExternalOutput").ap())
    encoder(nc, *args)
    r = run_bass_kernel_spmd(nc, [arrays], core_ids=[0])
    return tuple(r.results[0][f"out_{name}_dram"] for name in ("y_prompt", "y_sample"))
```
